# Optimizing a Trainium2 kernel written in Bass

```python
import math
import jax, jax.numpy as jnp
from jax import lax
import numpy as np

D_MODEL = 2048
BATCH = 1
SEQ = 512
DEPTH = 1
DEC_BATCH = 8
DEC_SEQ = 1
PAST_LEN = 4096
PAGE_SIZE = 128

SSD_HEADS = 16
SSD_HEAD_DIM = 64
SSD_WIDTH = SSD_HEADS * SSD_HEAD_DIM
SSD_GROUPS = 2
SSD_STATE = 128
SSD_CONV_DIM = SSD_WIDTH + 2 * SSD_GROUPS * SSD_STATE
GDN_HEADS = 8
GDN_HEAD_DIM = 128
GDN_WIDTH = GDN_HEADS * GDN_HEAD_DIM
GDN_CONV_DIM = 3 * GDN_WIDTH
MEM_TOKENS = 256
MEM_HEADS = 4
MEM_HEAD_DIM = 128
MEM_WIDTH = MEM_HEADS * MEM_HEAD_DIM

MIX_WIDTH = SSD_WIDTH + GDN_WIDTH + MEM_WIDTH
CONV_WIDTH = 4
CHUNK = 64
EPS = 1e-6
IN_SIZES = (SSD_CONV_DIM, SSD_HEADS, GDN_CONV_DIM, GDN_HEADS, GDN_HEADS, MEM_WIDTH, MIX_WIDTH)
IN_COLS = SSD_CONV_DIM + SSD_HEADS + GDN_CONV_DIM + 2 * GDN_HEADS + MEM_WIDTH + MIX_WIDTH

kernel_name = "hymba_ssd_gdn_memory_decoder_step"

def rmsnorm(x, w):
    xf = x.astype(jnp.float32)
    y = xf * lax.rsqrt(jnp.mean(xf * xf, axis=-1, keepdims=True) + EPS)
    return (y * w.astype(jnp.float32)).astype(x.dtype)

def headnorm(y):
    y = y.astype(jnp.float32)
    return y * lax.rsqrt(jnp.mean(y * y, axis=-1, keepdims=True) + EPS)

def l2norm(x):
    x = x.astype(jnp.float32)
    return x * lax.rsqrt(jnp.sum(x * x, axis=-1, keepdims=True) + EPS)

def pad_time(a, lp):
    pad = lp - a.shape[1]
    if pad == 0:
        return a
    widths = [(0, 0)] * a.ndim
    widths[1] = (0, pad)
    return jnp.pad(a, widths)

def causal_conv(prefix, u, w, b):
    L = u.shape[1]
    up = jnp.concatenate([prefix.astype(u.dtype), u], axis=1)
    out = up[:, 0:L] * w[0]
    for j in range(1, CONV_WIDTH):
        out = out + up[:, j:j + L] * w[j]
    if b is not None:
        out = out + b
    return jax.nn.silu(out), up[:, -(CONV_WIDTH - 1):]

def ssd_chunked(x, dt, A, Bm, Cm, D, h0):
    f32 = jnp.float32
    Bsz, L, H, P = x.shape
    G, N, R = SSD_GROUPS, SSD_STATE, H // SSD_GROUPS
    cs = min(CHUNK, L)
    nC = -(-L // cs)
    lp = nC * cs
    xc = pad_time(x.astype(f32), lp).reshape(Bsz, nC, cs, G, R, P)
    dtc = pad_time(dt.astype(f32), lp).reshape(Bsz, nC, cs, G, R)
    Bc = pad_time(Bm.astype(f32), lp).reshape(Bsz, nC, cs, G, N)
    Cc = pad_time(Cm.astype(f32), lp).reshape(Bsz, nC, cs, G, N)
    cum = jnp.cumsum(dtc * A.astype(f32).reshape(G, R), axis=2)
    cumT = jnp.moveaxis(cum, 2, -1)
    tril = jnp.tril(jnp.ones((cs, cs), bool))
    Lmat = jnp.exp(jnp.where(tril, cumT[..., :, None] - cumT[..., None, :], -jnp.inf))
    CB = jnp.einsum('bclgn,bcsgn->bcgls', Cc, Bc)
    scores = CB[:, :, :, None] * Lmat * jnp.moveaxis(dtc, 2, -1)[..., None, :]
    y = jnp.einsum('bcgrls,bcsgrp->bclgrp', scores, xc)
    cum_last = cum[:, :, -1]
    w_end = jnp.exp(cum_last[:, :, None] - cum) * dtc
    S = jnp.einsum('bcsgn,bcsgr,bcsgrp->bcgrpn', Bc, w_end, xc)

    def step(h, inp):
        dec, s = inp
        return h * jnp.exp(dec)[..., None, None] + s, h

    h0g = h0.astype(f32).reshape(Bsz, G, R, P, N)
    hT, h_prev = lax.scan(step, h0g, (jnp.moveaxis(cum_last, 1, 0), jnp.moveaxis(S, 1, 0)))
    h_prev = jnp.moveaxis(h_prev, 0, 1)
    y = y + jnp.einsum('bclgn,bcgrpn->bclgrp', Cc, h_prev) * jnp.exp(cum)[..., None]
    y = y + D.astype(f32).reshape(G, R)[:, :, None] * xc
    y = y.reshape(Bsz, lp, H, P)[:, :L]
    return y, hT.reshape(Bsz, H, P, N)

def gdn_chunked(q, k, v, g, beta, S0):
    f32 = jnp.float32
    Bsz, L, H, K = q.shape
    cs = min(CHUNK, L)
    nC = -(-L // cs)
    lp = nC * cs

    def blk(a):
        a = pad_time(a.astype(f32), lp)
        return jnp.moveaxis(a.reshape((Bsz, nC, cs, H) + a.shape[3:]), 3, 2)

    qc, kc, vc, gc, bc = blk(q), blk(k), blk(v), blk(g), blk(beta)
    Gc = jnp.cumsum(gc, axis=-1)
    tril = jnp.tril(jnp.ones((cs, cs), bool))
    eye = jnp.eye(cs, dtype=f32)
    decay = jnp.exp(jnp.where(tril, Gc[..., :, None] - Gc[..., None, :], -jnp.inf))
    kb = kc * bc[..., None]
    strict = tril & (eye == 0)
    Amat = jnp.where(strict, jnp.einsum('bnhik,bnhjk->bnhij', kb, kc) * decay, 0.0)
    T = lax.linalg.triangular_solve(eye + Amat, jnp.broadcast_to(eye, Amat.shape),
                                    left_side=True, lower=True, unit_diagonal=True)
    u = jnp.einsum('bnhij,bnhjv->bnhiv', T, vc * bc[..., None])
    wk = jnp.einsum('bnhij,bnhjk->bnhik', T, kb * jnp.exp(Gc)[..., None])
    attn = jnp.einsum('bnhik,bnhjk->bnhij', qc, kc) * decay
    qg = qc * jnp.exp(Gc)[..., None]
    g_last = Gc[..., -1]
    k_end = kc * jnp.exp(g_last[..., None] - Gc)[..., None]

    def step(S, inp):
        u_c, w_c, qg_c, a_c, ke_c, gl_c = inp
        v_new = u_c - jnp.einsum('bhik,bhkv->bhiv', w_c, S)
        o = jnp.einsum('bhik,bhkv->bhiv', qg_c, S) + jnp.einsum('bhij,bhjv->bhiv', a_c, v_new)
        S = S * jnp.exp(gl_c)[..., None, None] + jnp.einsum('bhjk,bhjv->bhkv', ke_c, v_new)
        return S, o

    mv = lambda a: jnp.moveaxis(a, 1, 0)
    ST, o = lax.scan(step, S0.astype(f32), (mv(u), mv(wk), mv(qg), mv(attn), mv(k_end), mv(g_last)))
    o = jnp.moveaxis(jnp.moveaxis(o, 0, 1), 2, 3)
    o = o.reshape(Bsz, lp, H, vc.shape[-1])[:, :L]
    return o, ST

def mixer(x, mem_k, mem_v, ssd_conv_prev, ssd_h, gdn_conv_prev, gdn_S,
          norm_w, w_in, ssd_conv_w, ssd_conv_b, ssd_dt_bias, ssd_A_log, ssd_D,
          gdn_conv_w, gdn_dt_bias, gdn_A_log, mix_norm_w, w_out):
    f32 = jnp.float32
    Bsz, L, _ = x.shape
    h = rmsnorm(x, norm_w)
    proj = jnp.einsum('bld,de->ble', h, w_in)
    splits = np.cumsum(IN_SIZES)[:-1].tolist()
    xbc_in, dt_raw, qkv_in, b_raw, a_raw, q_mem, z = jnp.split(proj, splits, axis=-1)

    xbc, ssd_conv_new = causal_conv(ssd_conv_prev, xbc_in, ssd_conv_w, ssd_conv_b)
    xs, Bm, Cm = jnp.split(xbc, [SSD_WIDTH, SSD_WIDTH + SSD_GROUPS * SSD_STATE], axis=-1)
    dt = jax.nn.softplus(dt_raw.astype(f32) + ssd_dt_bias.astype(f32))
    A = -jnp.exp(ssd_A_log.astype(f32))
    y_ssd, ssd_h_new = ssd_chunked(xs.reshape(Bsz, L, SSD_HEADS, SSD_HEAD_DIM), dt, A,
                                   Bm.reshape(Bsz, L, SSD_GROUPS, SSD_STATE),
                                   Cm.reshape(Bsz, L, SSD_GROUPS, SSD_STATE), ssd_D, ssd_h)

    qkv, gdn_conv_new = causal_conv(gdn_conv_prev, qkv_in, gdn_conv_w, None)
    q, k, v = jnp.split(qkv, [GDN_WIDTH, 2 * GDN_WIDTH], axis=-1)
    q = l2norm(q.reshape(Bsz, L, GDN_HEADS, GDN_HEAD_DIM)) * (GDN_HEAD_DIM ** -0.5)
    k = l2norm(k.reshape(Bsz, L, GDN_HEADS, GDN_HEAD_DIM))
    v = v.reshape(Bsz, L, GDN_HEADS, GDN_HEAD_DIM)
    beta = jax.nn.sigmoid(b_raw.astype(f32))
    g = -jnp.exp(gdn_A_log.astype(f32)) * jax.nn.softplus(a_raw.astype(f32) + gdn_dt_bias.astype(f32))
    y_gdn, gdn_S_new = gdn_chunked(q, k, v, g, beta, gdn_S)

    qm = q_mem.reshape(Bsz, L, MEM_HEADS, MEM_HEAD_DIM)
    s = jnp.einsum('blhd,bmhd->bhlm', qm, mem_k).astype(f32) * (MEM_HEAD_DIM ** -0.5)
    p = jax.nn.softmax(s, axis=-1)
    y_mem = jnp.einsum('bhlm,bmhd->blhd', p, mem_v.astype(f32))

    y = jnp.concatenate([headnorm(y_ssd).reshape(Bsz, L, SSD_WIDTH),
                         headnorm(y_gdn).reshape(Bsz, L, GDN_WIDTH),
                         headnorm(y_mem).reshape(Bsz, L, MEM_WIDTH)], axis=-1)
    y = y * mix_norm_w.astype(f32) * jax.nn.silu(z.astype(f32))
    out = jnp.einsum('ble,ed->bld', y.astype(x.dtype), w_out)
    return (x + out).astype(x.dtype), ssd_conv_new, ssd_h_new, gdn_conv_new, gdn_S_new

def setup_inputs(seed: int = 0) -> dict:
    key = jax.random.key(seed)
    ks = jax.random.split(key, 24)
    f32 = jnp.float32

    def nrm(k, shape, s=1.0):
        return s * jax.random.normal(k, shape, f32)

    def unif(k, shape, lo, hi):
        return jax.random.uniform(k, shape, f32, lo, hi)

    def dt_bias(k, shape):
        dt = jnp.exp(unif(k, shape, math.log(1e-3), math.log(1e-1)))
        return dt + jnp.log(-jnp.expm1(-dt))

    return {
        "x_prompt": nrm(ks[0], (BATCH, SEQ, D_MODEL)),
        "x_sample": nrm(ks[1], (DEC_BATCH, DEC_SEQ, D_MODEL)),
        "mem_prompt": nrm(ks[2], (BATCH, MEM_TOKENS, D_MODEL)),
        "state_ssd_conv": nrm(ks[3], (DEPTH, DEC_BATCH, CONV_WIDTH - 1, SSD_CONV_DIM)),
        "state_ssd": nrm(ks[4], (DEPTH, DEC_BATCH, SSD_HEADS, SSD_HEAD_DIM, SSD_STATE), 0.1),
        "state_gdn_conv": nrm(ks[5], (DEPTH, DEC_BATCH, CONV_WIDTH - 1, GDN_CONV_DIM)),
        "state_gdn": nrm(ks[6], (DEPTH, DEC_BATCH, GDN_HEADS, GDN_HEAD_DIM, GDN_HEAD_DIM), 0.1),
        "cache_mem_k": nrm(ks[7], (DEPTH, DEC_BATCH, MEM_TOKENS, MEM_HEADS, MEM_HEAD_DIM)),
        "cache_mem_v": nrm(ks[8], (DEPTH, DEC_BATCH, MEM_TOKENS, MEM_HEADS, MEM_HEAD_DIM)),
        "norm_w": 1.0 + nrm(ks[9], (DEPTH, D_MODEL), 0.02),
        "w_in": nrm(ks[10], (DEPTH, D_MODEL, IN_COLS), D_MODEL ** -0.5),
        "ssd_conv_w": nrm(ks[11], (DEPTH, CONV_WIDTH, SSD_CONV_DIM), CONV_WIDTH ** -0.5),
        "ssd_conv_b": nrm(ks[12], (DEPTH, SSD_CONV_DIM), 0.02),
        "ssd_dt_bias": dt_bias(ks[13], (DEPTH, SSD_HEADS)),
        "ssd_A_log": jnp.log(unif(ks[14], (DEPTH, SSD_HEADS), 1.0, 16.0)),
        "ssd_D": 1.0 + nrm(ks[15], (DEPTH, SSD_HEADS), 0.1),
        "gdn_conv_w": nrm(ks[16], (DEPTH, CONV_WIDTH, GDN_CONV_DIM), CONV_WIDTH ** -0.5),
        "gdn_dt_bias": dt_bias(ks[17], (DEPTH, GDN_HEADS)),
        "gdn_A_log": jnp.log(unif(ks[18], (DEPTH, GDN_HEADS), 1.0, 16.0)),
        "mem_norm_w": 1.0 + nrm(ks[19], (DEPTH, D_MODEL), 0.02),
        "w_mem_kv": nrm(ks[20], (DEPTH, D_MODEL, 2 * MEM_WIDTH), D_MODEL ** -0.5),
        "mix_norm_w": 1.0 + nrm(ks[21], (DEPTH, MIX_WIDTH), 0.02),
        "w_out": nrm(ks[22], (DEPTH, MIX_WIDTH, D_MODEL), MIX_WIDTH ** -0.5),
        "final_norm_w": 1.0 + nrm(ks[23], (D_MODEL,), 0.02),
    }

def reference(x_prompt, x_sample, mem_prompt, state_ssd_conv, state_ssd, state_gdn_conv, state_gdn,
              cache_mem_k, cache_mem_v, norm_w, w_in, ssd_conv_w, ssd_conv_b, ssd_dt_bias, ssd_A_log,
              ssd_D, gdn_conv_w, gdn_dt_bias, gdn_A_log, mem_norm_w, w_mem_kv, mix_norm_w, w_out,
              final_norm_w):
    f32 = jnp.float32
    Bp = x_prompt.shape[0]
    xp, xs = x_prompt, x_sample
    p_sc, p_sh, p_gc, p_gs, p_mk, p_mv = [], [], [], [], [], []
    s_sc, s_sh, s_gc, s_gs = [], [], [], []
    for l in range(DEPTH):
        lp = (norm_w[l], w_in[l], ssd_conv_w[l], ssd_conv_b[l], ssd_dt_bias[l], ssd_A_log[l], ssd_D[l],
              gdn_conv_w[l], gdn_dt_bias[l], gdn_A_log[l], mix_norm_w[l], w_out[l])
        kv = jnp.einsum('bmd,de->bme', rmsnorm(mem_prompt, mem_norm_w[l]), w_mem_kv[l])
        mk, mv = jnp.split(kv, 2, axis=-1)
        mk = mk.reshape(Bp, MEM_TOKENS, MEM_HEADS, MEM_HEAD_DIM)
        mv = mv.reshape(Bp, MEM_TOKENS, MEM_HEADS, MEM_HEAD_DIM)
        xp, sc, sh, gc, gs = mixer(
            xp, mk, mv,
            jnp.zeros((Bp, CONV_WIDTH - 1, SSD_CONV_DIM), xp.dtype),
            jnp.zeros((Bp, SSD_HEADS, SSD_HEAD_DIM, SSD_STATE), f32),
            jnp.zeros((Bp, CONV_WIDTH - 1, GDN_CONV_DIM), xp.dtype),
            jnp.zeros((Bp, GDN_HEADS, GDN_HEAD_DIM, GDN_HEAD_DIM), f32), *lp)
        p_sc.append(sc); p_sh.append(sh); p_gc.append(gc); p_gs.append(gs); p_mk.append(mk); p_mv.append(mv)
        xs, sc, sh, gc, gs = mixer(xs, cache_mem_k[l], cache_mem_v[l], state_ssd_conv[l], state_ssd[l],
                                   state_gdn_conv[l], state_gdn[l], *lp)
        s_sc.append(sc); s_sh.append(sh); s_gc.append(gc); s_gs.append(gs)
    y_prompt = rmsnorm(xp, final_norm_w)
    y_sample = rmsnorm(xs, final_norm_w)
    p_ssd_conv = jnp.stack(p_sc); p_ssd = jnp.stack(p_sh)
    p_gdn_conv = jnp.stack(p_gc); p_gdn = jnp.stack(p_gs)
    p_mem_k = jnp.stack(p_mk); p_mem_v = jnp.stack(p_mv)
    s_ssd_conv = jnp.stack(s_sc); s_ssd = jnp.stack(s_sh)
    s_gdn_conv = jnp.stack(s_gc); s_gdn = jnp.stack(s_gs)
    return (y_prompt, y_sample, p_ssd_conv, p_ssd, p_gdn_conv, p_gdn, p_mem_k, p_mem_v,
            s_ssd_conv, s_ssd, s_gdn_conv, s_gdn)


_drawn_inputs = setup_inputs


def setup_inputs(seed=0):
    import zlib

    import numpy as np

    out = dict(_drawn_inputs(seed))
    spreads = {}
    factors = {'ssd_D': 58.368, 'mem_norm_w': 8.467, 'mix_norm_w': 16.161, 'final_norm_w': 8.264}
    for name, (base, spread) in spreads.items():
        noise = np.random.default_rng([zlib.crc32(name.encode()), seed]).standard_normal(out[name].shape)
        drawn = base * np.exp(spread * noise) if base else spread * noise
        out[name] = __import__('jax').numpy.asarray(drawn.astype(out[name].dtype))
    for name, factor in factors.items():
        out[name] = (out[name] * factor).astype(out[name].dtype)
    return out
```

```python
from contextlib import ExitStack

import numpy as np

import concourse.bass as bass
from concourse import mybir
from concourse.alu_op_type import AluOpType as ALU

F32 = mybir.dt.float32
F32R = mybir.dt.float32r
BF16 = mybir.dt.bfloat16
BYTES = {F32: 4, F32R: 4, BF16: 2}
ACT = mybir.ActivationFunctionType
AX = mybir.AxisListType.X

P = 128
D = 2048
KT = D // P
SEQ = 512
DB = 8
NT = DB + SEQ
HALF = NT // 2
NC = SEQ // P
EPS = 1e-6
SSD_H, SSD_P, SSD_G, SSD_N = 16, 64, 2, 128
SSD_W = SSD_H * SSD_P
SSD_CONV = SSD_W + 2 * SSD_G * SSD_N
GDN_H = 8
GDN_W = GDN_H * P
GDN_CONV = 3 * GDN_W
MEM_T, MEM_H = 256, 4
MEM_W = MEM_H * P
MIX = SSD_W + GDN_W + MEM_W
ET = MIX // P
CW = 4
COL_DT = SSD_CONV
COL_QKV = COL_DT + SSD_H
COL_B = COL_QKV + GDN_CONV
COL_QM = COL_B + 2 * GDN_H
COL_Z = COL_QM + MEM_W
N_SSD_T = SSD_CONV // P
N_GDN_T = GDN_CONV // P
NCONV = N_SSD_T + N_GDN_T
SM = SSD_H + 2 * GDN_H
UNIT = 1024
NRAW = 3
LEVELS = [1, 2, 4, 8, 16, 32, 64]
SLOT = [8 + e for e in range(8)] + [e - 8 for e in range(8, 16)] + list(range(16, 20))

TILES = [("ssd", i, P * i) for i in range(N_SSD_T)]
for _j in range(3):
    TILES.append(("gdn", _j * GDN_H, COL_QKV + P * _j * GDN_H))
TILES += [("qm", i, COL_QM + P * i) for i in range(MEM_H)]
for _h in range(1, GDN_H):
    for _j in range(3):
        TILES.append(("gdn", _j * GDN_H + _h, COL_QKV + P * (_j * GDN_H + _h)))
TILES += [("z", e, COL_Z + P * e) for e in range(ET)]
NTILE = len(TILES)
CONV_SEQ = [n for n, t in enumerate(TILES) if t[0] in ("ssd", "gdn")]
QM_SEQ = [n for n, t in enumerate(TILES) if t[0] == "qm"]
Z_SEQ = [n for n, t in enumerate(TILES) if t[0] == "z"]
FIN_V = 10
N_UNITS = KT + 2 * NTILE + KT * ET // 8
GSTEPS = 30
PAUSE = ("pause",)
PAUSES = {
    "ssd 1": 1, "ssdend": 1, "gdn 0": 1, "gdn 1": 2, "gdn 3": 2, "gdn 18": 1, "gdn 22": 1, "gdn 29": 8, "att 1": 1, "decssd0": 3,
    "decbc": 1, "decssd": 1, "decssdy": 3, "decgdn 0": 1, "decattp": 6, "decatty": 1, "decnorm": 1,
}
CARRY = 20
POOL_TILES = (12, 50)
FIRST = 19
VEC_SIZES = (KT, KT, ET, NCONV * CW, N_SSD_T, SM, SM, SSD_H, SSD_H // 2)
NVEC = sum(VEC_SIZES)

GROUPS = {
    "setup_pe": [("small_ps", 1), ("small_done", 1), ("cum_done", 1)],
    "setup_act": [("a_done", 1), ("sp_exp", 1), ("sp_ln", 1), ("beta_done", 1), ("e_da_done", 1), ("e_cum_done", 1),
                  ("e_tot_done", 1), ("w_end_exp", 1)],
    "setup_dve": [("eps_set", 2), ("ident_r", 1), ("wsm_split", 2), ("hist_step", 5), ("small_copied", 1), ("sp_abs", 1),
                  ("sp_done", 1), ("da_done", 1), ("cum_copied", 2), ("w_end_diff", 1), ("row0", 2),
                  ("w_end_done", 1), ("masks_done", 1), ("mv_done", 2)],
    "norm_act": [("rstd_ln", 1), ("rstd", 1)],
    "ssd_pe": [("s_turned", 1), ("s_stateps", 1)],
    "ssd_act": [("s_bcopy", 2), ("s_exp", 4), ("s_ysq", 1), ("s_yln", 1), ("s_yr", 1)],
    "ssd_inter_dve": [("s_inter_read", 1), ("s_inter_add", 1)],
    "ssd_end_dve": [("s_intra_read", 1), ("s_state_new", 1), ("s_red", 1), ("s_y_normed", 1)],
    "gdn_pe": [("g_turned", 1), ("g_rows", 1), ("g_gram", 1), ("g_t0_ps", 1), ("g_tf_ps", 1), ("g_res_ps", 1),
               ("g_fix_ps", 1), ("g_wt_ps", 1), ("g_y_turned", 1)],
    "gdn_act": [("g_sq", 8), ("g_ln", 1), ("g_ea", 1), ("g_ke", 1), ("g_qrow", 1), ("g_exp", 2),
                ("g_tf", 1), ("g_wt", 1), ("g_vcopy", 4), ("g_ysq", 1), ("g_yln", 1), ("g_yr", 1),
                ("g_y_copied", 1)],
    "gdn_dve": [("g_rowx", 1), ("g_row", 1), ("g_col", 1), ("g_colt", 1), ("g_scaled", 3), ("g_sub", 2),
                ("g_qg", 1), ("g_nat", 1), ("g_attn", 1), ("g_tt0", 1), ("g_resx", 1), ("g_res", 1), ("g_ttf", 1),
                ("g_state", 4), ("g_y_ss", 1), ("g_y_scaled", 1)],
    "att_pe": [("a_scores", 1), ("a_turned", 1), ("a_y_ps", 1)],
    "att_act": [("a_exp", 1), ("a_pt", 1)],
    "att_dve": [("a_max", 1), ("a_nmax", 1)],
    "att_y_act": [("a_ysq", 1), ("a_yln", 1), ("a_yr", 1), ("a_y_copied", 1)],
    "att_y_dve": [("a_rec", 1), ("a_y_div", 1), ("a_y_ss", 1), ("a_y_scaled", 1)],
    "dec_pe": [("d_k_ps", 1), ("d_bb_ps", 2), ("d_ss_ps", 1), ("d_sc_ps", 8), ("d_pt_ps", 1), ("d_pv", 8),
               ("d_yt_ps", 1), ("d_yss", 1)],
    "dec_act": [("d_k", 1), ("d_bb", 4), ("d_sq", 2), ("d_ln", 2), ("d_g", 1), ("d_pexp", 1), ("d_yt", 1),
                ("y_dec_mem", 1), ("d_ysq", 1), ("d_yln", 2), ("d_yr", 1)],
    "dec_dve": [("d_wide", 2), ("d_dtx", 1), ("d_sqv", 1), ("d_sel", 2), ("d_kq", 2), ("d_qk", 2), ("d_qsel", 1), ("d_max", 1),
                ("d_nmax", 1), ("d_rec", 1), ("d_p", 1), ("d_psel", 1), ("d_ynorm", 1), ("dec_gated", 6)],
    "dec_ssd_dve": [("d_ymul", 1), ("d_yred", 1), ("y_dec_ssd", 1)],
    "dec_gdn_pe": [("d_ks", 1), ("d_vb", 1)],
    "dec_gdn_dve": [("d_ks_read", 2), ("d_vsub", 1), ("d_vn", 1), ("d_vqk", 1), ("y_dec_gdn", 1), ("d_outer", 1)],
    "fin_act": [("fin_ln", 1), ("fin_r", 1)],
}
GROUP_OF = {event: group for group, events in GROUPS.items() for event, _ in events}


def spread(main, side):
    out, done = [], 0
    for i, item in enumerate(main):
        out.append(item)
        upto = (i + 1) * len(side) // len(main)
        out += [s for s in side[done:upto] if s != PAUSE]
        done = upto
    return out


def paced(side):
    out = []
    for it in side:
        step = f"{it[0]} {it[-1]}" if it[0] in ("ssd", "gdn", "att", "atty", "decgdn") else it[0]
        out += [PAUSE] * PAUSES.get(step, 0) + [it]
    return out


def proj_items(first, last):
    out = []
    for n in range(first, last):
        for k in range(KT):
            out.append(("proj", n, k))
            if k in (1, 4, 6, 8, 10, 12) and n > 0:
                out.append(("post", n - 1, (1, 4, 6, 8, 10, 12).index(k)))
    return out


def timeline():
    items = [("const",)] + [("xsq", k) for k in range(KT)] + [("xrstd",)]
    items += [("xh", k) for k in range(8)] + spread(proj_items(0, 1)[:8], [("xh", k) for k in range(8, KT)]) + [("setup",)]
    items += proj_items(0, 1)[8:] + [("small",)]
    a, b = N_SSD_T, N_SSD_T + 3 + MEM_H
    msq = [("msq", k) for k in range(KT)]
    early = [PAUSE, ("smallturn",), PAUSE, PAUSE, ("smallpost",)] + msq[:4] + [("smallpost2",)] + msq[4:10]
    early += [("smallcum",), msq[10], ("smallend",)] + msq[11:] + [("mrstd",)] + [PAUSE] * 5 + [("mh", k) for k in range(KT)]
    items += spread(proj_items(1, 4), early)
    for it in proj_items(4, a):
        items.append(it)
        if it[0] == "proj" and it[2] % 8 == 7:
            items.append(("kv", 2 * (it[1] - 4) + it[2] // 8))
    items += [("kvout",)]
    side = [("ssd", c, s) for c in range(NC) for s in range(9)] + [("ssdend",)]
    start = proj_items(a, b)
    items += start[:FIRST] + spread(start[FIRST:], paced(side))
    for h in range(GDN_H):
        main = proj_items(b + 3 * h, b + 3 * (h + 1))
        before = [("gdn", h - 1, s) for s in range(CARRY, GSTEPS)] if h else []
        items += spread(main[:FIRST], paced(before)) + spread(main[FIRST:], paced([("gdn", h, s) for s in range(CARRY)]))
    late = [("gdn", GDN_H - 1, s) for s in range(CARRY, GSTEPS)]
    for h in range(MEM_H):
        for c in range(NC):
            late += [("att", h, c, 0), ("att", h, c, 1)]
            if c == 0 and h:
                late += [("atty", h - 1, 1)]
            late += [("att", h, c, 2)]
        late += [("atty", h, 0)]
    late += [("atty", MEM_H - 1, 1), ("decssd0",)]
    for g in range(SSD_G):
        late += [("decbc", g)]
        for i in range(4 * g, 4 * g + 4):
            late += [("decssd", i), ("decssdy", i)]
    late += [("decgdn0",)] + [("decgdn", h, s) for h in range(GDN_H) for s in range(2)]
    late += [("decattk", i) for i in range(DB)] + [("decatts",), ("decattp",)] + [("decattv", i) for i in range(DB)]
    late += [("decatty", 0), ("decatty", 1), ("decnorm",), ("decgate", 0), ("decgate", 1)]
    items += spread(proj_items(b + 3 * GDN_H, NTILE - 1), paced(late))
    items += spread(proj_items(NTILE - 1, NTILE), [("yhi", e) for e in range(ET - 4)])
    items += [("ylo", 0), ("ylo", 1), ("post", NTILE - 1, 0), ("ylo", 2), ("ylo", 3), ("out", 0, 0), ("post", NTILE - 1, 1),
              ("out", 0, 1), ("post", NTILE - 1, 2), ("out", 0, 2), ("decgate", 2), ("ylo", 4), ("ylo", 5)]
    items += spread([("out", 0, e) for e in (3, 4, 5)], [("yhi", e) for e in range(ET - 4, ET)])
    for n in range(KT):
        for e in range(ET):
            if n == 0 and e < 6:
                continue
            if n == 0:
                items.append(("ylo", e))
            items.append(("out", n, e))
            if n and e in (1, 4, 7, 10):
                items.append(("fin", n - 1, (1, 4, 7, 10).index(e)))
    items += [("fin", KT - 1, s) for s in range(4)] + [("final",)]
    return items


def ring_order(items):
    order = {}
    for it in items:
        if it[0] == "kv" or it[0] == "proj" and it[2] % 8 == 0 or it[0] == "out" and (ET * it[1] + it[2]) % 8 == 0:
            order[it] = len(order)
    return order


def build(nc, I, O):
    ctx = ExitStack()
    sems = {}

    def sem(name):
        name = GROUP_OF.get(name, name)
        if name not in sems:
            sems[name] = ctx.enter_context(nc.semaphore(name))
        return sems[name]

    def upto(name, times):
        group = GROUP_OF.get(name)
        if group is None:
            return sem(name), times
        before = 0
        for other, each in GROUPS[group]:
            if other == name:
                break
            before += each
        turn, place_in_turn = divmod(times - 1, each)
        return sem(name), turn * sum(n for _, n in GROUPS[group]) + before + place_in_turn + 1

    base = [16512]

    def at(name, shape, dt, offset):
        return nc.alloc_sbuf_tensor_at(name, shape, dt, offset=offset)

    def place(name, shape, dt=F32):
        t = at(name, shape, dt, base[0])
        base[0] += (int(np.prod(shape[1:])) * BYTES[dt] + 31) // 32 * 32
        return t

    class Region:

        def __init__(self, size):
            self.start, self.next, self.end = base[0], base[0], base[0] + size
            base[0] += (size + 31) // 32 * 32

        def reset(self, to=None):
            self.next = self.start if to is None else to

        def place(self, name, shape, dt=F32):
            t = at(name, shape, dt, self.next)
            self.next += (int(np.prod(shape[1:])) * BYTES[dt] + 31) // 32 * 32
            assert self.next <= self.end, name
            return t

    r_h = Region(2 * KT * NT * 4)
    h_hi = r_h.place("h_hi", [P, KT, NT], F32R)
    h_lo = r_h.place("h_lo", [P, KT, NT], F32R)
    r_y = Region(ET * NT * 4)
    r_side = Region(ET * NT * 4)
    raw = place("w_raw", [P, NRAW, UNIT])
    w_hi = place("w_hi", [P, 2, UNIT], F32R)
    w_lo = place("w_lo", [P, 2, UNIT], F32R)
    conv_u = place("conv_u", [P, 2, NT])
    conv_a = place("conv_a", [P, 2, NT])
    csts = place("csts", [P, 3, P])
    triu, ones, blocks = (csts[:, i, :] for i in range(3))
    ident_r = place("ident_r", [P, P], F32R)
    ident = ident_r[:, :].bitcast(F32)
    masks = place("masks", [P, len(LEVELS), P], BF16)
    vecs = place("vecs", [P, NVEC])
    at_vec = 0
    parts = []
    for n in VEC_SIZES:
        parts.append(vecs[:, at_vec:at_vec + n])
        at_vec += n
    norm_w, mem_norm_w, mix_w, conv_w, conv_b, sm_bias, sm_a, sm_d, d_lay = parts
    conv_w = conv_w.rearrange("p (t j) -> p t j", j=CW)
    hist3 = place("hist3", [P, NCONV, DB, 3])
    hist = place("hist", [P, NCONV, DB])
    tails = place("tails", [P, NCONV, 3])
    dec = place("dec", [P, NCONV + MEM_H, DB])
    z_dec = place("z_dec", [P, ET, DB])
    y_dec = place("y_dec", [P, ET, DB])
    da = place("da", [P, 5, SM])
    sp = place("sp", [P, 5, SM])
    cum = place("cum", [P, NC, SM])
    tot = place("tot", [P, NC, SM])
    e_cum = place("e_cum", [P, NC, SSD_H])
    w_end = place("w_end", [P, NC, SSD_H])
    e_tot = place("e_tot", [P, NC, SM])
    beta = place("beta", [P, 5, GDN_H])
    row_a0 = place("row_a0", [P, NC, GDN_H])
    row_q0 = place("row_q0", [P, NC, GDN_H])
    e_da = place("e_da", [P, SM])
    eps = place("eps", [P, 2])
    g_row = place("g_row", [P, 2, NC])
    g_s = place("g_s", [P, 6, 8])
    r_b = Region(8192)
    att_s = place("att_s", [P, 8, MEM_H * NC])
    assert base[0] <= 229344, base[0]

    x_t = at("x_t", [P, KT, NT], F32, r_y.start)
    mem_t = at("mem_t", [P, KT // 2, MEM_T], F32, r_b.start)
    mem_t2 = at("mem_t2", [P, KT // 2, MEM_T], F32, r_y.start + KT * NT * 4)
    mem_hi = r_side.place("mem_hi", [P, KT, MEM_T], F32R)
    mem_lo = r_side.place("mem_lo", [P, KT, MEM_T], F32R)
    wsm_hi = r_side.place("wsm_hi", [P, KT, SM], F32R)
    wsm_lo = r_side.place("wsm_lo", [P, KT, SM], F32R)
    early_end = r_side.next
    wsm_raw = r_side.place("wsm_raw", [P, KT, SM])
    hist_tmp = r_side.place("hist_tmp", [P, NCONV, DB])
    r_side.reset(early_end)
    m_w = r_side.place("m_w", [P, 2, MEM_T])
    m_rstd = r_side.place("m_rstd", [P, MEM_T])
    m_sq = m_w
    masks_f = at("masks_f", [P, len(LEVELS), P], F32, r_y.start)
    sp_all = at("sp_all", [P, 6, 5, SM], F32, r_y.start + 2 * NT * 4)
    sp_t = [sp_all[:, i, :, :] for i in range(6)]
    sm_t = at("sm_t", [P, NT], F32, r_y.start + 4 * NT * 4)
    ident_f = att_s[:, :, :].rearrange("p a b -> p (a b)")
    x_w = conv_u
    x_sq = (conv_u, conv_a)
    x_rstd = conv_a[:, 0, :]

    r_b.reset()
    mk_t = r_b.place("mk_t", [P, MEM_H, MEM_T])
    mv = r_b.place("mv", [P, 2, MEM_W])
    y_raw = at("y_raw", [P, ET, NT], F32, r_y.start)
    bc = y_raw[:, 4:8, :]

    r_side.reset()
    gconv = r_side.place("gconv", [P, 3, NT])
    after_conv = r_side.next
    s_xdt = r_side.place("s_xdt", [P, SSD_W])
    s_xw = r_side.place("s_xw", [P, SSD_W])
    s_y = r_side.place("s_y", [P, 2, SSD_W])
    s_tmp = r_side.place("s_tmp", [P, SSD_W])
    s_btok = r_side.place("s_btok", [P, SSD_G, P])
    s_cb = r_side.place("s_cb", [P, SSD_G, P])
    s_l = r_side.place("s_l", [P, 2, 4, P])
    s_state = r_side.place("s_state", [P, SSD_W])
    s_red = r_side.place("s_red", [P, 3, SSD_H])

    r_side.reset(after_conv)
    g_e_at = (r_side.next + 6 * NC * P * 4, r_side.next + 7 * NC * P * 4)
    g_r1, g_r2, g_kend, g_natf, g_attn, g_qg, g_e1, g_e2, g_tf, g_res, g_ttf, g_wt = (
        r_side.place(f"g_{n}", [P, NC, P]) for n in "r1 r2 kend natf attn qg e1 e2 tf res ttf wt".split())
    g_t, g_tt, g_p = (r_side.place(f"g_{n}", [P, NC, P], F32R) for n in "t tt p".split())
    g_natm = [at(f"g_natm{i}", [P, NC, P], F32R, e_start) for i, e_start in enumerate(g_e_at)]
    state_a = r_side.place("state_a", [P, 2, P])
    vnew = r_side.place("vnew", [P, 2, P])

    r_side.reset(r_side.start + 4 * DB * P * 4)
    a_y = r_side.place("a_y", [P, NC, P])
    a_sq = r_side.place("a_sq", [P, NC, P])
    att_p = r_side.place("att_p", [P, 2, MEM_T])
    att_pt = r_side.place("att_pt", [P, 2, 2, P])

    r_side.reset()
    d_st = r_side.place("d_st", [P, 4, DB, P])
    d_bb = r_side.place("d_bb", [P, 2, DB, P])
    d_tmp = r_side.place("d_tmp", [P, DB, P])
    d_tmp2 = r_side.place("d_tmp2", [P, DB, P])
    d_k = r_side.place("d_k", [P, 3, 8, DB])
    d_sq = r_side.place("d_sq", [P, 3, GDN_H, DB])
    d_ln = r_side.place("d_ln", [P, 2, GDN_H, DB])
    d_kq = r_side.place("d_kq", [P, GDN_H, DB, 2])
    d_g = r_side.place("d_g", [P, 3, GDN_H, DB])
    d_sel = r_side.place("d_sel", [P, 2, GDN_H, DB])
    d_v = r_side.place("d_v", [P, 4, DB])
    d_p = r_side.place("d_p", [P, 2, P])
    pairs = DB * MEM_H
    q_sel = at("q_sel", [P, pairs * pairs], F32, r_side.start + 4 * DB * P * 4)
    p_sel = at("p_sel", [P, 2, pairs * pairs], F32, r_side.start + 6 * DB * P * 4)
    d_sv = r_side.place("d_sv", [P, 4])
    d_n = r_side.place("d_n", [P, 2, ET, DB])

    r_side.reset()
    y_hi = r_side.place("y_hi", [P, ET, NT], F32R)
    y_lo = at("y_lo", [P, ET, NT], F32R, r_h.start)
    fin = at("fin", [P, KT, NT], F32, r_y.start)
    r_h.reset(r_h.start + ET * NT * 4)
    fin_w = r_h.place("fin_w", [P, KT])
    fin_sq = r_h.place("fin_sq", [P, 2, NT])
    fin_acc = r_h.place("fin_acc", [P, NT])
    fin_r = r_h.place("fin_r", [P, NT])

    ps = ctx.enter_context(nc.psum_tensor("ps", [P, 8, 512], F32))
    side = [ps[:, 4 + i, :] for i in range(4)]

    def proj_ps(n):
        b = 2 * (n % 2)
        return ps[:, b:b + 2, 0:HALF]

    def halves(ap):
        return ap.rearrange("p (j t) -> p j t", j=2)

    def flat4(t):
        return t[:, :, :].rearrange("p c t -> p (c t)")

    def quad(ap):
        return ap.rearrange("p (c t) -> p c t", c=4)

    def heads(ap):
        if len(ap.shape) == 3:
            ap = ap.rearrange("p b q -> p (b q)")
        return ap.rearrange("p (h q) -> p h q", h=SSD_H)

    def along(ap, n):
        return ap.unsqueeze(len(ap.shape)).to_broadcast(list(ap.shape) + [n])

    def across(ap, m):
        return ap.unsqueeze(1).to_broadcast([ap.shape[0], m, ap.shape[1]])

    def chunk(c):
        return slice(DB + P * c, DB + P * c + P)

    items = timeline()
    ring = ring_order(items)

    def unit_of(it):
        if it[0] == "kv":
            return ring[it], 0
        if it[0] == "proj":
            return ring["proj", it[1], it[2] // 8 * 8], it[2] % 8
        m = ET * it[1] + it[2]
        return ring[("out",) + divmod(m // 8 * 8, ET)], m % 8

    def tile_units(n):
        return ring["proj", n, 8] + 1

    kv_units = ring["kv", KT - 1] + 1
    in_units = tile_units(NTILE - 1)
    pool_units = range(ring["proj", POOL_TILES[0], 0], ring["proj", POOL_TILES[1], 0])

    def low_part(g, pieces):
        if g in pool_units:
            return sem("w_lo_pool"), 2 * (g - pool_units[0]) + pieces
        return sem("w_lo_done"), 2 * (g - (len(pool_units) if g > pool_units[-1] else 0)) + pieces
    conv_at = {n: i for i, n in enumerate(CONV_SEQ)}
    z_at = {n: i for i, n in enumerate(Z_SEQ)}
    block = ctx.enter_context(nc.Block())

    def conv_index(n):
        kind, i, _ = TILES[n]
        return i if kind == "ssd" else N_SSD_T + i

    @block.sync
    def _(spe):
        sources = {}
        for it, r in ring.items():
            if it[0] == "kv":
                sources[r] = I["w_mem"][it[1]]
            elif it[0] == "proj":
                sources[r] = I["w_in"][2 * it[1] + it[2] // 8]
            else:
                sources[r] = I["w_out"][(ET * it[1] + it[2]) // 8]

        def load_unit(r):
            if r >= N_UNITS:
                return
            if r >= NRAW:
                spe.wait_ge(*upto("w_hi_done", 2 * (r - NRAW + 1)))
                spe.wait_ge(*low_part(r - NRAW, 2))
            spe.dma_start(raw[:, r % NRAW, :], sources[r]).then_inc(sem(f"w_in{r % NRAW}"), 16)

        def load_residual(j):
            spe.dma_start(fin[:, 2 * j:2 * j + 2, :], I["x_t"][:, 2 * j:2 * j + 2, :]).then_inc(sem(f"res_in{j % 2}"), 16)

        for it in items:
            k = it[0]
            if k == "const":
                spe.dma_start(csts[:, :, :], I["csts"]).then_inc(sem("csts_in"), 16)
                for j in range(8):
                    spe.dma_start(x_t[:, 2 * j:2 * j + 2, :], I["x_t"][:, 2 * j:2 * j + 2, :]).then_inc(sem(f"x_in{j}"), 16)
                spe.dma_start(vecs[:, :], I["vecs"]).then_inc(sem("vecs_in"), 16)
                load_unit(0)
                spe.dma_start(ident_f, I["ident"]).then_inc(sem("ident_in"), 16)
                load_unit(1)
                spe.dma_start(wsm_raw[:, :, :], I["w_small"]).then_inc(sem("wsm_in"), 16)
                spe.dma_start(hist3[:, :, :, :], I["hist"]).then_inc(sem("hist_in"), 16)
                load_unit(2)
                spe.dma_start(mem_t[:, :, :], I["mem_t"][:, 0:KT // 2, :]).then_inc(sem("mem_in"), 16)
                spe.dma_start(mem_t2[:, :, :], I["mem_t"][:, KT // 2:, :]).then_inc(sem("mem2_in"), 16)
            elif k == "small":
                spe.wait_ge(*upto("x_w", KT))
                spe.dma_start(masks_f[:, :, :], I["masks"]).then_inc(sem("masks_in"), 16)
            elif k == "kvout":
                spe.wait_ge(*upto("mk_done", 2))
                spe.wait_ge(*upto("mv_done", 2))
                spe.dma_start(O["p_mem_k"], mk_t[:, :, :]).then_inc(sem("out_mk"), 16)
                spe.dma_start(O["p_mem_v"], mv[:, :, :]).then_inc(sem("out_mv"), 16)
            if it in ring:
                load_unit(ring[it] + NRAW)
            if k == "out" and it[1] == 0 and it[2] == ET - 1:
                spe.wait_ge(*upto("y_hi_done", ET))
                spe.wait_ge(*upto("y_lo_g", ET // 2))
                spe.wait_ge(*upto("y_lo_v", ET // 2))
                spe.dma_start(fin_w[:, :], I["final_w"]).then_inc(sem("fin_w_in"), 16)
                load_residual(0)
                load_residual(1)
            if k == "out" and it[2] == 12 and it[1] % 2 == 1 and it[1] <= KT - 5:
                spe.wait_ge(*upto("fin_added", it[1]))
                load_residual((it[1] + 3) // 2)
            if k == "final":
                for n in range(0, KT, 2):
                    spe.wait_ge(*upto("scaled_v" if n < FIN_V else "scaled_g", (n if n < FIN_V else n - FIN_V) + 2))
                    spe.dma_start(O["y_t"][:, n:n + 2, :], fin[:, n:n + 2, :]).then_inc(sem("out_y"), 16)
        spe.wait_ge(*upto("out_mk", 16))
        spe.wait_ge(*upto("out_mv", 16))
        spe.wait_ge(*upto("out_y", 16 * KT // 2))
        spe.wait_ge(*upto("out_tails", 32))
        spe.wait_ge(*upto("out_pssd", 16))
        spe.wait_ge(*upto("out_pgdn", 16 * GDN_H))
        for j in range(4):
            spe.wait_ge(sem(f"out_st{j}"), 16 * 4)

    @block.tensor
    def _(pe):
        mm = nc.tensor.matmul
        turn = nc.tensor.transpose

        def unit_ready(g):
            pe.wait_ge(*upto("w_hi_done", 2 * (g + 1)))
            pe.wait_ge(*low_part(g, 2))

        def one(out, lhs, rhs):
            return mm(out, lhs, rhs, start=True, stop=True)

        def ssd_intra(c, qd):
            pe.wait_ge(*upto("s_scores", 4 * c + qd + 1))
            if c > 0 and qd == 0:
                pe.wait_ge(*upto("s_inter_read", c))
            if c == 0 and qd == 0:
                pe.wait_ge(*upto("s_x_read", 3))
            for j in range(4):
                h = 4 * qd + j
                last = one(heads(ps[:, 4:6, :])[:, h, :], s_l[:, qd % 2, j, :], s_xdt[:, SSD_P * h:SSD_P * h + SSD_P])
            last.then_inc(sem("s_intra"), 1)

        def ssd_turn_y(c):
            pe.wait_ge(*upto("s_y_normed", c + 1))
            pe.wait_ge(*upto("s_state_new", c + 1))
            if c + 1 < NC:
                pe.wait_ge(*upto("s_bcopy", 2 * (c + 2)))
            for i in range(8):
                last = turn(ps[:, 6:8, :].rearrange("p b (i t) -> p (b i) t", i=4)[:, i, :], s_y[:, c % 2, P * i:P * i + P], ident)
            last.then_inc(sem("s_y_turned"), 1)

        for it in items:
            k = it[0]
            if k == "xsq" and it[1] % 2 == 1:
                kk = it[1]
                if kk == 1:
                    pe.wait_ge(*upto("csts_in", 16))
                pe.wait_ge(*upto("x_sq_sum", (kk + 1) // 2))
                for hf in range(2):
                    last = mm(side[hf][:, 0:HALF], ones, x_sq[kk // 2 % 2][:, 0, HALF * hf:HALF * hf + HALF], start=kk == 1, stop=kk == KT - 1)
                last.then_inc(sem("x_sq_used"), 1)
            elif k == "msq":
                kk = it[1]
                pe.wait_ge(*upto("m_sq", kk + 1))
                mm(side[1][:, 0:MEM_T], ones, m_sq[:, kk % 2, :], start=kk == 0, stop=kk == KT - 1).then_inc(sem("m_sq_used"), 1)
            elif k == "kv":
                kk = it[1]
                g = ring[it]
                unit_ready(g)
                if kk == 0:
                    pe.wait_ge(*upto("m_hi", KT))
                    pe.wait_ge(*upto("m_lo", KT))
                hi, lo = w_hi[:, g % 2, :], w_lo[:, g % 2, :]
                for h in range(MEM_H):
                    out = side[h // 2][:, MEM_T * (h % 2):MEM_T * (h % 2) + MEM_T]
                    cols = slice(P * h, P * h + P)
                    for j, (w, a) in enumerate(((hi, mem_hi), (hi, mem_lo), (lo, mem_hi))):
                        last = mm(out, w[:, cols], a[:, kk, :], start=(kk == 0 and j == 0 and h % 2 == 0),
                                  stop=(kk == KT - 1 and j == 2), skip_group_check=True)
                for m in range(2):
                    for j, (a, w) in enumerate(((mem_hi, hi), (mem_hi, lo), (mem_lo, hi))):
                        last = mm(side[2 + m], a[:, kk, P * m:P * m + P], w[:, MEM_W:], start=(kk == 0 and j == 0),
                                  stop=(kk == KT - 1 and j == 2))
                last.then_inc(sem("unit_used"), 1)
            elif k == "small":
                pe.wait_ge(*upto("x_lo_v", KT // 2))
                pe.wait_ge(*upto("x_lo_g", KT // 2))
                pe.wait_ge(*upto("wsm_split", 2))
                for kk in range(KT):
                    for j, (w, a) in enumerate(((wsm_hi, h_hi), (wsm_hi, h_lo), (wsm_lo, h_hi))):
                        for hf in range(2):
                            last = mm(side[hf][0:SM, 0:HALF], w[:, kk, :], a[:, kk, HALF * hf:HALF * hf + HALF],
                                      start=(kk == 0 and j == 0), stop=(kk == KT - 1 and j == 2))
                last.then_inc(sem("small_ps"), 1)
            elif k == "smallturn":
                pe.wait_ge(*upto("small_copied", 1))
                for t in range(5):
                    cols = chunk(t) if t < NC else slice(0, P)
                    last = turn(side[3][:, SM * t:SM * t + SM], sm_t[0:SM, cols], ident[0:SM, 0:SM])
                last.then_inc(sem("small_done"), 1)
            elif k == "smallcum":
                pe.wait_ge(*upto("da_done", 1))
                rhs = da[:, 0:NC, :].rearrange("p c h -> p (c h)")
                one(side[2][:, 0:P], triu, rhs)
                one(side[2][:, P:2 * P], ones, rhs).then_inc(sem("cum_done"), 1)
            elif k == "proj":
                n, kk = it[1], it[2]
                g, b = unit_of(it)
                if b == 0:
                    unit_ready(g)
                if n == 0:
                    pe.wait_ge(*upto("x_hi", kk + 1))
                    pe.wait_ge(*upto("x_lo_v" if kk % 2 else "x_lo_g", kk // 2 + 1))
                if kk == 0 and n >= 2:
                    pe.wait_ge(*upto("tile_read", n - 1))
                out = proj_ps(n)
                hi = w_hi[:, g % 2, P * b:P * b + P]
                lo = w_lo[:, g % 2, P * b:P * b + P]
                for j, (w, a) in enumerate(((hi, h_hi), (hi, h_lo), (lo, h_hi))):
                    for hf in range(2):
                        last = mm(out[:, hf, :], w, a[:, kk, HALF * hf:HALF * hf + HALF],
                                  start=(kk == 0 and j == 0), stop=(kk == KT - 1 and j == 2))
                if b == 7:
                    last.then_inc(sem("unit_used"), 1)
            elif k == "ssd":
                c, s = it[1], it[2]
                if s == 0:
                    if c == 0:
                        pe.wait_ge(*upto("conv_out", N_SSD_T))
                        pe.wait_ge(*upto("mk_done", 2))
                        pe.wait_ge(*upto("mv_done", 2))
                    else:
                        pe.wait_ge(*upto("s_intra_read", c))
                        pe.wait_ge(*upto("s_state_new", c))
                    xs = ps[:, 4:6, :].rearrange("p b (i t) -> p (b i) t", i=4)
                    for i in range(8):
                        turn(xs[:, i, :], y_raw[:, 8 + i, chunk(c)], ident)
                    for g in range(SSD_G):
                        turn(side[2][:, P * g:P * g + P], bc[:, g, chunk(c)], ident)
                    for g in range(SSD_G):
                        last = one(side[2][:, P * (2 + g):P * (3 + g)], bc[:, g, chunk(c)], bc[:, 2 + g, chunk(c)])
                    last.then_inc(sem("s_turned"), 1)
                elif s == 1 and c > 0:
                    pe.wait_ge(*upto("s_x_read", 3 * (c + 1)))
                    for g in range(SSD_G):
                        last = one(side[g], bc[:, 2 + g, chunk(c)], s_state[:, 512 * g:512 * g + 512])
                    last.then_inc(sem("s_inter"), 1)
                    ssd_turn_y(c - 1)
                if 2 <= s <= 5:
                    qd = s - 2
                    if qd == 0 and c > 0:
                        pe.wait_ge(*upto("s_y_copied", c))
                    if qd > 0:
                        pe.wait_ge(*upto("s_sub", 4 * c + qd))
                    if qd == 0 and c == 0:
                        pe.wait_ge(*upto("cum_copied", 2))
                    for j in range(4):
                        h = 4 * qd + j
                        last = one(side[3][:, P * j:P * j + P], cum[:, c, h:h + 1].to_broadcast([P, P]), ident)
                    last.then_inc(sem("s_rows"), 1)
                if 3 <= s <= 6:
                    ssd_intra(c, s - 3)
                if s == 6:
                    pe.wait_ge(*upto("s_bcopy", 2 * (c + 1)))
                    pe.wait_ge(*upto("s_sub", 4 * (c + 1)))
                    for g in range(SSD_G):
                        last = one(side[2 + g], s_btok[:, g, :], s_xw[:, 512 * g:512 * g + 512])
                    last.then_inc(sem("s_stateps"), 1)
            elif k == "ssdend":
                ssd_turn_y(NC - 1)
            elif k == "gdn":
                h, s = it[1], it[2]
                q, kk_, v = (gconv[:, j, :] for j in range(3))
                if s == 0:
                    pe.wait_ge(*upto("conv_out", N_SSD_T + 3 * (h + 1)))
                    if h == 0:
                        pe.wait_ge(*upto("s_y_copied", NC))
                        pe.wait_ge(*upto("s_intra_read", NC))
                        pe.wait_ge(*upto("s_state_new", NC))
                    else:
                        pe.wait_ge(*upto("g_y_copied", h))
                        pe.wait_ge(*upto("g_vcopy", 4 * h))
                        pe.wait_ge(*upto("g_y_scaled", h))
                    for c in range(NC):
                        turn(quad(side[0])[:, c, :], kk_[:, chunk(c)], ident)
                    for c in range(NC):
                        turn(quad(side[2])[:, c, :], q[:, chunk(c)], ident)
                    for c in range(NC):
                        last = turn(quad(side[1])[:, c, :], v[:, chunk(c)], ident)
                    last.then_inc(sem("g_turned"), 1)
                elif s == 1:
                    pe.wait_ge(*upto("g_row", h + 1))
                    for i in range(2):
                        for c in range(NC):
                            last = one(quad(side[2 + i])[:, c, :], g_row[:, i, c:c + 1].to_broadcast([P, P]), ident)
                    last.then_inc(sem("g_rows"), 1)
                elif s == 2:
                    pe.wait_ge(*upto("g_scaled", 3 * (h + 1)))
                    for c in range(NC):
                        one(quad(side[0])[:, c, :], kk_[:, chunk(c)], kk_[:, chunk(c)])
                    for c in range(NC):
                        last = one(quad(side[1])[:, c, :], kk_[:, chunk(c)], q[:, chunk(c)])
                    last.then_inc(sem("g_gram"), 1)
                elif s == 3:
                    pe.wait_ge(*upto("g_natm", 7 * h + 1))
                    for c in range(NC):
                        last = one(quad(side[0])[:, c, :], g_natm[0][:, c, :], ident_r[:, :])
                    last.then_inc(sem("g_t0_ps"), 1)
                elif 4 <= s < 16:
                    level, second = divmod(s - 2, 2)
                    if second == 0:
                        pe.wait_ge(*upto("g_t_new", 6 * h + level))
                        pe.wait_ge(*upto("g_natm", 7 * h + level + 1))
                        if level == 1:
                            pe.wait_ge(*upto("g_attn", h + 1))
                        for c in range(NC):
                            last = one(quad(side[1])[:, c, :], g_natm[level % 2][:, c, :], g_t[:, c, :])
                        last.then_inc(sem("g_at"), 1)
                    else:
                        pe.wait_ge(*upto("g_p", 6 * h + level))
                        if level == 1:
                            pe.wait_ge(*upto("g_qrow", h + 1))
                            pe.wait_ge(*upto("g_sub", 2 * (h + 1)))
                        else:
                            pe.wait_ge(*upto("g_tt_new", 6 * h + level - 1))
                        for c in range(NC):
                            last = one(quad(side[3])[:, c, :], g_p[:, c, :], g_tt[:, c, :])
                        if level < 6:
                            for c in range(NC):
                                last = one(quad(side[2])[:, c, :], g_tt[:, c, :], g_p[:, c, :])
                        last.then_inc(sem("g_tat"), 1)
                elif s == 16:
                    pe.wait_ge(*upto("g_tt_new", 6 * h + 6))
                    pe.wait_ge(*upto("g_t_new", 6 * h + 6))
                    for c in range(NC):
                        last = turn(quad(side[0])[:, c, :], g_tt[:, c, :].bitcast(F32), ident)
                    last.then_inc(sem("g_tf_ps"), 1)
                elif s == 17:
                    pe.wait_ge(*upto("g_tf", h + 1))
                    pe.wait_ge(*upto("g_p", 6 * h + 6))
                    for c in range(NC):
                        last = one(quad(side[1])[:, c, :], g_natf[:, c, :], g_tf[:, c, :])
                    last.then_inc(sem("g_res_ps"), 1)
                elif s == 18:
                    pe.wait_ge(*upto("g_res", h + 1))
                    for c in range(NC):
                        last = one(quad(side[2])[:, c, :], g_res[:, c, :], g_tt[:, c, :].bitcast(F32))
                    last.then_inc(sem("g_fix_ps"), 1)
                elif s == 19:
                    pe.wait_ge(*upto("g_ttf", h + 1))
                    for c in range(NC):
                        last = one(quad(side[3])[:, c, :], g_r2[:, c, :], g_ttf[:, c, :])
                    last.then_inc(sem("g_wt_ps"), 1)
                elif 20 <= s < 28:
                    c, second = divmod(s - 20, 2)
                    if second == 0:
                        if c == 0:
                            pe.wait_ge(*upto("g_wt", h + 1))
                        else:
                            pe.wait_ge(*upto("g_state", 4 * h + c))
                        out = side[c % 2][:, 0:P]
                        last = mm(out, g_ttf[:, c, :], g_r1[:, c, :], start=True, stop=c == 0)
                        if c:
                            last = mm(out, g_wt[:, c, :], state_a[:, (c - 1) % 2, :], start=False, stop=True)
                        last.then_inc(sem("g_v_ps"), 1)
                    else:
                        pe.wait_ge(*upto("g_vcopy", 4 * h + c + 1))
                        vn = vnew[:, c % 2, :]
                        one(side[3][:, 0:P], g_kend[:, c, :], vn)
                        last = mm(quad(side[2])[:, c, :], g_attn[:, c, :], vn, start=True, stop=c == 0)
                        if c:
                            last = mm(quad(side[2])[:, c, :], g_qg[:, c, :], state_a[:, (c - 1) % 2, :], start=False, stop=True)
                        last.then_inc(sem("g_o_ps"), 1)
                elif s == 29:
                    pe.wait_ge(*upto("g_y_scaled", h + 1))
                    pe.wait_ge(*upto("g_state", 4 * h + 4))
                    for c in range(NC):
                        last = turn(quad(side[3])[:, c, :], g_res[:, c, :], ident)
                    last.then_inc(sem("g_y_turned"), 1)
            elif k == "att":
                h, c, s = it[1:]
                i = NC * h + c
                if s == 0:
                    if i == 0:
                        pe.wait_ge(*upto("g_y_copied", GDN_H))
                        pe.wait_ge(*upto("g_y_scaled", GDN_H))
                        pe.wait_ge(*upto("g_vcopy", 4 * GDN_H))
                        pe.wait_ge(*upto("tile_read", QM_SEQ[-1] + 1))
                    if i >= 2:
                        pe.wait_ge(*upto("a_exp", i - 1))
                    one(side[i % 2][:, 0:MEM_T], y_raw[:, 16 + h, chunk(c)], mk_t[:, h, :]).then_inc(sem("a_scores"), 1)
                elif s == 1:
                    pe.wait_ge(*upto("a_exp", i + 1))
                    if i >= 2:
                        pe.wait_ge(*upto("a_pt", i - 1))
                    for m in range(2):
                        last = turn(side[2][:, 256 * (i % 2) + P * m:256 * (i % 2) + P * m + P], att_p[:, i % 2, P * m:P * m + P], ident)
                    last.then_inc(sem("a_turned"), 1)
                else:
                    pe.wait_ge(*upto("a_pt", i + 1))
                    if c == 0 and h > 0:
                        pe.wait_ge(*upto("a_y_copied", h))
                    for m in range(2):
                        last = mm(quad(side[3])[:, c, :], att_pt[:, i % 2, m, :], mv[:, m, P * h:P * h + P], start=m == 0, stop=m == 1)
                    last.then_inc(sem("a_y_ps"), 1)
            elif k == "atty" and it[2] == 1:
                h = it[1]
                pe.wait_ge(*upto("a_y_scaled", h + 1))
                for c in range(NC):
                    last = turn(quad(side[3])[:, c, :], a_y[:, c, :], ident)
                last.then_inc(sem("a_y_turned"), 1)
            elif k == "decssd0":
                pe.wait_ge(*upto("d_wide", 2))
                pe.wait_ge(*upto("a_exp", MEM_H * NC))
                for v, src in enumerate((d_tmp, d_tmp2)):
                    for t in range(8):
                        last = one(side[0][:, 64 * v + 8 * t:64 * v + 8 * t + 8], src[0:DB, t, :], ident[0:DB, 0:DB])
                last.then_inc(sem("d_k_ps"), 1)
            elif k == "decbc":
                g = it[1]
                if g == 0:
                    pe.wait_ge(*upto("d_k", 1))
                    pe.wait_ge(*upto("a_y_copied", MEM_H))
                    pe.wait_ge(*upto("a_pt", MEM_H * NC))
                else:
                    pe.wait_ge(*upto("d_bb", 2 * g))
                for j in range(2):
                    for b in range(DB):
                        last = one(quad(side[2 * j + b // 4])[:, b % 4, :], dec[:, 8 + 2 * j + g, b:b + 1].to_broadcast([P, P]), ident)
                last.then_inc(sem("d_bb_ps"), 1)
            elif k == "decgdn0":
                pe.wait_ge(*upto("d_sq", 2))
                pe.wait_ge(*upto("d_sqv", 1))
                pe.wait_ge(*upto("d_sel", 2))
                pe.wait_ge(*upto("d_bb", 4))
                flat = d_sq[:, :, :, :].rearrange("p a h b -> p (a h b)")
                one(side[0][:, 0:3 * 64], ones, flat)
                one(side[0][:, 192:320], ones[0:DB, :], d_sel[0:DB, :, :, :].rearrange("p a h b -> p (a h b)")).then_inc(sem("d_ss_ps"), 1)
            elif k == "decgdn" and it[2] == 0:
                h = it[1]
                pe.wait_ge(sem(f"st_in{h % 4}"), 16 * (2 + h // 4 + 1))
                if h == 0:
                    pe.wait_ge(*upto("d_kq", 2))
                else:
                    pe.wait_ge(*upto("d_ks_read", 2 * h))
                for b in range(DB):
                    last = one(side[1][:, 2 * b:2 * b + 2], d_st[:, h % 4, b, :], d_kq[:, h, b, :])
                last.then_inc(sem("d_ks"), 1)
            elif k == "decgdn":
                h = it[1]
                pe.wait_ge(*upto("d_vn", h + 1))
                if h:
                    pe.wait_ge(*upto("d_outer", h))
                for b in range(DB):
                    last = one(quad(side[2 + b // 4])[:, b % 4, :], d_v[:, 2, b:b + 1].to_broadcast([P, P]), ident)
                last.then_inc(sem("d_vb"), 1)
            elif k == "decattk":
                b = it[1]
                pe.wait_ge(sem(f"st_in{b % 4}"), 16 * (4 + b // 4 + 1))
                if b == 0:
                    pe.wait_ge(*upto("d_qsel", 1))
                for h in range(MEM_H):
                    i = MEM_H * b + h
                    last = mm(side[0][0:pairs, 0:MEM_T], q_sel[:, pairs * i:pairs * i + pairs],
                              d_st[:, b % 4, 2 * h:2 * h + 2, :].rearrange("p m t -> p (m t)"), start=i == 0, stop=i == pairs - 1)
                last.then_inc(sem("d_sc_ps"), 1)
            elif k == "decattp":
                pe.wait_ge(*upto("d_p", 1))
                pe.wait_ge(*upto("d_outer", GDN_H))
                for m in range(2):
                    last = turn(side[2][:, pairs * m:pairs * m + pairs], d_p[0:pairs, m, :], ident[0:pairs, 0:pairs])
                last.then_inc(sem("d_pt_ps"), 1)
            elif k == "decattv":
                b = it[1]
                pe.wait_ge(sem(f"st_in{b % 4}"), 16 * (6 + b // 4 + 1))
                if b == 0:
                    pe.wait_ge(*upto("d_psel", 1))
                for h in range(MEM_H):
                    i = MEM_H * b + h
                    for m in range(2):
                        last = mm(side[3][0:pairs, 0:P], p_sel[:, m, pairs * i:pairs * i + pairs], d_st[:, b % 4, 4 * m + h, :],
                                  start=(i == 0 and m == 0), stop=(i == pairs - 1 and m == 1))
                last.then_inc(sem("d_pv"), 1)
            elif k == "decatty" and it[1] == 1:
                pe.wait_ge(*upto("d_yt", 1))
                turn(side[2][:, 0:pairs], d_p[0:pairs, 0, :], ident[0:pairs, 0:pairs]).then_inc(sem("d_yt_ps"), 1)
            elif k == "decnorm":
                pe.wait_ge(*upto("d_ysq", 1))
                pe.wait_ge(*upto("d_pexp", 1))
                sq = d_n[:, 0, :, :].rearrange("p e b -> p (e b)")
                one(side[0][:, 0:64], blocks, sq[:, 0:64])
                one(side[0][:, 64:160], ones, sq[:, 64:160]).then_inc(sem("d_yss"), 1)
            elif k == "out":
                n, e = it[1], it[2]
                g, b = unit_of(it)
                if b == 0:
                    unit_ready(g)
                if n == 0:
                    pe.wait_ge(*upto("y_hi_done", e + 1))
                    pe.wait_ge(*upto("y_lo_v" if e % 2 else "y_lo_g", e // 2 + 1))
                if e == 0:
                    if n < 2:
                        pe.wait_ge(*upto("tile_read", NTILE - 1 + n))
                    elif n >= 2:
                        pe.wait_ge(*upto("fin_added", n - 1))
                out = proj_ps(NTILE + n)
                hi = w_hi[:, g % 2, P * b:P * b + P]
                lo = w_lo[:, g % 2, P * b:P * b + P]
                for j, (w, a) in enumerate(((hi, y_hi), (hi, y_lo), (lo, y_hi))):
                    for hf in range(2):
                        last = mm(out[:, hf, :], w, a[:, SLOT[e], HALF * hf:HALF * hf + HALF],
                                  start=(e == 0 and j == 0), stop=(e == ET - 1 and j == 2))
                if b == 7:
                    last.then_inc(sem("unit_used"), 1)
                elif e == ET - 1:
                    last.then_inc(sem("out_ps"), 1)
            elif k == "final":
                pe.wait_ge(*upto("fin_acc", KT - 1))
                for hf in range(2):
                    mm(side[hf][:, 0:HALF], ones, fin_acc[:, HALF * hf:HALF * hf + HALF], start=True, stop=False)
                pe.wait_ge(*upto("fin_sq", KT))
                for hf in range(2):
                    last = mm(side[hf][:, 0:HALF], ones, fin_sq[:, (KT - 1) % 2, HALF * hf:HALF * hf + HALF], start=False, stop=True)
                last.then_inc(sem("fin_ss"), 1)

    @block.scalar
    def _(act):
        A = nc.scalar.activation

        def split_hi(g, piece):
            if g >= N_UNITS:
                return
            if piece == 0:
                act.wait_ge(sem(f"w_in{g % NRAW}"), 16 * (g // NRAW + 1))
                if g >= 2:
                    act.wait_ge(*upto("unit_used", g - 1))
            s = slice(512 * piece, 512 * piece + 512)
            A(w_hi[:, g % 2, s], raw[:, g % NRAW, s], ACT.Copy).then_inc(sem("w_hi_done"), 1)

        def state_load(i):
            if i >= 32:
                return
            slot = d_st[:, i % 4, :, :]
            kind, j = divmod(i, 8)
            if i >= 4:
                pk, pj = divmod(i - 4, 8)
                if pk == 0:
                    act.wait_ge(sem(f"out_st{i % 4}"), 16 * (pj // 4 + 1))
                    act.wait_ge(*upto("d_ymul", pj + 1))
                elif pk == 1:
                    act.wait_ge(sem(f"out_st{i % 4}"), 16 * (2 + pj // 4 + 1))
                elif pk == 2:
                    act.wait_ge(*upto("d_sc_ps", pj + 1))
                else:
                    act.wait_ge(*upto("d_pv", pj + 1))
            src = I[("st_ssd", "st_gdn", "c_k", "c_v")[kind]][j]
            act.dma_start(slot, src).then_inc(sem(f"st_in{i % 4}"), 16)

        def state_step(n):
            if 2 <= n < 18:
                state_store(*divmod(n - 2, 8))
            if n >= 3:
                state_load(n + 1)

        def state_store(kind, j):
            name = ("s_ssd", "s_gdn")[kind]
            act.wait_ge(*upto("d_new", 8 * kind + j + 1))
            act.dma_start(O[name][j], d_st[:, j % 4, :, :]).then_inc(sem(f"out_st{j % 4}"), 16)

        for it in items:
            k = it[0]
            if k == "const":
                act.wait_ge(*upto("eps_set", 2))
            elif k == "xsq":
                kk = it[1]
                act.wait_ge(sem(f"x_in{kk // 2}"), 16)
                if kk >= 4:
                    act.wait_ge(*upto("x_sq_used", kk // 2 - 1))
                A(x_sq[kk // 2 % 2][:, kk % 2, :], x_t[:, kk, :], ACT.Square).then_inc(sem("x_sq"), 1)
                if kk == KT - 1:
                    split_hi(0, 0)
                    split_hi(0, 1)
            elif k == "xrstd":
                act.wait_ge(*upto("x_sq_used", KT // 2))
                A(halves(x_rstd), ps[:, 4:6, 0:HALF], ACT.Ln, scale=1.0 / D, bias=eps[:, 0:1]).then_inc(sem("rstd_ln"), 1)
                act.wait_ge(*upto("rstd_ln", 1))
                A(x_rstd, x_rstd, ACT.Exp, scale=-0.5).then_inc(sem("rstd"), 1)
                split_hi(1, 0)
                split_hi(1, 1)
            elif k == "xh":
                kk = it[1]
                act.wait_ge(*upto("x_w", kk + 1))
                A(h_hi[:, kk, :], x_w[:, kk % 2, :], ACT.Copy).then_inc(sem("x_hi"), 1)
            elif k == "msq":
                kk = it[1]
                if kk == 0:
                    act.wait_ge(*upto("hist_step", 5))
                act.wait_ge(*upto("mem_in" if kk < 8 else "mem2_in", 16))
                if kk >= 2:
                    act.wait_ge(*upto("m_sq_used", kk - 1))
                A(m_sq[:, kk % 2, :], mem_t[:, kk, :] if kk < 8 else mem_t2[:, kk - 8, :], ACT.Square).then_inc(sem("m_sq"), 1)
            elif k == "mrstd":
                act.wait_ge(*upto("m_sq_used", KT))
                A(m_rstd[:, :], side[1][:, 0:MEM_T], ACT.Ln, scale=1.0 / D, bias=eps[:, 0:1]).then_inc(sem("rstd_ln"), 1)
                act.wait_ge(*upto("rstd_ln", 2))
                A(m_rstd[:, :], m_rstd[:, :], ACT.Exp, scale=-0.5).then_inc(sem("rstd"), 1)
            elif k == "mh":
                kk = it[1]
                act.wait_ge(*upto("m_w", kk + 1))
                A(mem_hi[:, kk, :], m_w[:, kk % 2, :], ACT.Copy).then_inc(sem("m_hi"), 1)
            elif k == "kv":
                split_hi(ring[it] + 1, 0)
                split_hi(ring[it] + 1, 1)
            elif k == "kvout":
                act.wait_ge(*upto("unit_used", kv_units))
                for j in range(2):
                    A(mk_t[:, 2 * j:2 * j + 2, :], side[j].rearrange("p (h m) -> p h m", h=2), ACT.Copy).then_inc(sem("mk_done"), 1)
            elif k == "smallpost":
                act.wait_ge(*upto("vecs_in", 16))
                A(sm_a, sm_a, ACT.Exp).then_inc(sem("a_done"), 1)
                act.wait_ge(*upto("sp_abs", 1))
                A(sp_t[1], sp_t[0], ACT.Exp, scale=-1.0).then_inc(sem("sp_exp"), 1)
                act.wait_ge(*upto("sp_exp", 1))
                A(sp_t[2], sp_t[1], ACT.Ln, bias=eps[:, 1:2]).then_inc(sem("sp_ln"), 1)
            elif k == "smallpost2":
                act.wait_ge(*upto("sp_done", 1))
                A(beta[:, :, :], sp[:, :, SSD_H:SSD_H + GDN_H], ACT.Exp, scale=-1.0).then_inc(sem("beta_done"), 1)
                act.wait_ge(*upto("da_done", 1))
                A(e_da[:, :], da[:, 4, :], ACT.Exp).then_inc(sem("e_da_done"), 1)
            elif k == "smallend":
                act.wait_ge(*upto("cum_copied", 2))
                A(e_cum[:, :, :], cum[:, :, 0:SSD_H], ACT.Exp).then_inc(sem("e_cum_done"), 1)
                A(e_tot[:, :, :], tot[:, :, :], ACT.Exp).then_inc(sem("e_tot_done"), 1)
                act.wait_ge(*upto("w_end_diff", 1))
                A(w_end[:, :, :], w_end[:, :, :], ACT.Exp).then_inc(sem("w_end_exp"), 1)
            elif k == "proj" and it[2] % 8 in (0, 3):
                g, b = unit_of(it)
                if g:
                    split_hi(g + 1, 0 if b == 0 else 1)
            elif k == "post":
                n, s = it[1], it[2]
                kind, i, _ = TILES[n]
                if s == 0:
                    act.wait_ge(*upto("unit_used", tile_units(n)))
                if kind in ("ssd", "gdn"):
                    ci, sq = conv_index(n), conv_at[n]
                    b = sq % 2
                    if s == 0:
                        if sq < 2:
                            act.wait_ge(*upto("x_lo_v", KT // 2))
                            act.wait_ge(*upto("x_lo_g", KT // 2))
                        else:
                            act.wait_ge(*upto("tap_done", 4 * (sq - 1)))
                            act.wait_ge(*upto("tail_done", 2 * (sq - 1)))
                            act.wait_ge(*upto("conv_out", sq - 1))
                        A(halves(conv_u[:, b, :]), proj_ps(n), ACT.Copy).then_inc(sem("conv_u"), 1)
                        bias = conv_b[:, i:i + 1] if kind == "ssd" else 0.0
                        A(halves(conv_a[:, b, :]), proj_ps(n), ACT.Identity, scale=conv_w[:, ci, 3:4], bias=bias).then_inc(sem("tile_read"), 1)
                    elif s == 5:
                        act.wait_ge(*upto("tap_done", 4 * (sq + 1)))
                        if kind == "ssd":
                            dst = y_raw[:, 8 + i if i < 8 else i - 4, :]
                        else:
                            h = (sq - N_SSD_T) // 3
                            dst = gconv[:, (sq - N_SSD_T) % 3, :]
                            if h >= 1:
                                act.wait_ge(*upto("g_gram", h))
                                act.wait_ge(*upto("g_qg", h))
                            else:
                                act.wait_ge(*upto("unit_used", kv_units))
                        A(dst, conv_a[:, b, :], ACT.Silu)
                        A(dec[:, ci, :], conv_a[:, b, 0:DB], ACT.Silu).then_inc(sem("conv_out"), 1)
                elif kind == "qm":
                    if s == 0:
                        A(halves(y_raw[:, 16 + i, :]), proj_ps(n), ACT.Copy)
                        A(dec[:, NCONV + i, :], proj_ps(n)[:, 0, 0:DB], ACT.Copy).then_inc(sem("tile_read"), 1)
                elif kind == "z" and s == 0:
                    zi = z_at[n]
                    b = zi % 2
                    if zi < 2:
                        act.wait_ge(*upto("conv_out", NCONV))
                        act.wait_ge(*upto("tap_done", 4 * NCONV))
                    else:
                        act.wait_ge(*upto("z_gated", zi - 1))
                        act.wait_ge(*upto("z_dec", zi - 1))
                    A(halves(conv_a[:, b, :]), proj_ps(n), ACT.Silu).then_inc(sem("tile_read"), 1)
            elif k == "ssd":
                c, s = it[1], it[2]
                if s == 0:
                    act.wait_ge(*upto("s_turned", c + 1))
                    if c:
                        act.wait_ge(*upto("s_stateps", c))
                        act.wait_ge(*upto("s_scores", 4 * c))
                    A(s_btok[:, :, :].rearrange("p g n -> p (g n)"), side[2][:, 0:256], ACT.Copy).then_inc(sem("s_bcopy"), 1)
                    A(s_cb[:, :, :].rearrange("p g n -> p (g n)"), side[2][:, 256:512], ACT.Copy).then_inc(sem("s_bcopy"), 1)
                elif s == 1 and c > 0:
                    act.wait_ge(*upto("s_y_turned", c))
                    A(y_raw[:, 8:16, chunk(c - 1)], ps[:, 6:8, :].rearrange("p b (i t) -> p (b i) t", i=4), ACT.Copy).then_inc(sem("s_y_copied"), 1)
                if 2 <= s <= 5:
                    i = 4 * c + s - 2
                    act.wait_ge(*upto("s_masked", i + 1))
                    A(s_l[:, i % 2, :, :], s_l[:, i % 2, :, :], ACT.Exp).then_inc(sem("s_exp"), 1)
                if s == 7:
                    act.wait_ge(*upto("s_intra_read", c + 1))
                    if c:
                        act.wait_ge(*upto("s_red", c))
                    A(s_tmp[:, :], s_y[:, c % 2, :], ACT.Square).then_inc(sem("s_ysq"), 1)
                if s == 8:
                    act.wait_ge(*upto("s_red", c + 1))
                    A(s_red[:, 1, :], s_red[:, 0, :], ACT.Ln, scale=1.0 / SSD_P, bias=eps[:, 0:1]).then_inc(sem("s_yln"), 1)
                    act.wait_ge(*upto("s_yln", c + 1))
                    if c:
                        act.wait_ge(*upto("s_y_normed", c))
                    A(s_red[:, 2, :], s_red[:, 1, :], ACT.Exp, scale=-0.5).then_inc(sem("s_yr"), 1)
                    if c == NC - 1:
                        act.wait_ge(*upto("s_state_new", NC))
                        act.dma_start(O["p_ssd"], s_state[:, :]).then_inc(sem("out_pssd"), 16)
            elif k == "ssdend":
                act.wait_ge(*upto("s_y_turned", NC))
                A(y_raw[:, 8:16, chunk(NC - 1)], ps[:, 6:8, :].rearrange("p b (i t) -> p (b i) t", i=4), ACT.Copy).then_inc(sem("s_y_copied"), 1)
            elif k == "gdn":
                h, s = it[1], it[2]
                if s == 0:
                    act.wait_ge(*upto("conv_out", N_SSD_T + 3 * (h + 1)))
                    if h == 0:
                        act.wait_ge(*upto("s_state_new", NC))
                        act.wait_ge(*upto("s_y_normed", NC))
                        act.wait_ge(*upto("s_y_turned", NC))
                        act.wait_ge(*upto("s_intra", 4 * NC))
                        act.wait_ge(*upto("out_pssd", 16))
                    else:
                        act.wait_ge(*upto("g_y_ss", h))
                        act.wait_ge(*upto("g_attn", h))
                    act.wait_ge(*upto("g_turned", h + 1))
                    for i, (e, bank) in enumerate(((g_e1, side[2]), (g_e2, side[0]))):
                        for c in range(NC):
                            A(e[:, c, :], quad(bank)[:, c, :], ACT.Square, accum_out=g_s[:, 1, 4 * i + c:4 * i + c + 1]).then_inc(sem("g_sq"), 1)
                    if h:
                        act.wait_ge(*upto("g_col", h))
                    act.wait_ge(*upto("g_sq", 8 * (h + 1)))
                    A(g_s[:, 0, :], g_s[:, 1, :], ACT.Ln, bias=eps[:, 0:1]).then_inc(sem("g_ln"), 1)
                    act.wait_ge(*upto("g_row", h + 1))
                    A(g_s[:, 3, 0:4], g_row[:, 0, :], ACT.Exp).then_inc(sem("g_ea"), 1)
                    act.wait_ge(*upto("g_colt", h + 1))
                    A(g_s[:, 4, 0:4], g_s[:, 4, 0:4], ACT.Exp).then_inc(sem("g_ke"), 1)
                elif s == 1:
                    act.wait_ge(*upto("g_rows", h + 1))
                    if h:
                        act.wait_ge(*upto("g_o_ps", 4 * h))
                    act.wait_ge(*upto("g_sub", 2 * h + 2))
                    A(g_qg[:, :, :], quad(side[3]), ACT.Exp).then_inc(sem("g_qrow"), 1)
                    act.wait_ge(*upto("g_masked", 2 * h + 1))
                    A(g_e1[:, :, :], g_e1[:, :, :], ACT.Exp).then_inc(sem("g_exp"), 1)
                    act.wait_ge(*upto("g_masked", 2 * h + 2))
                    A(g_e2[:, :, :], g_e2[:, :, :], ACT.Exp).then_inc(sem("g_exp"), 1)
                elif 4 <= s < 16 and s % 2 == 1:
                    act.wait_ge(*upto("g_tat", 6 * h + (s - 3) // 2))
                    A(g_tt[:, :, :], quad(side[3]), ACT.Copy).then_inc(sem("g_tt_new"), 1)
                elif s == 16:
                    act.wait_ge(*upto("g_tf_ps", h + 1))
                    if h:
                        act.wait_ge(*upto("g_res", h))
                    A(g_tf[:, :, :], quad(side[0]), ACT.Copy).then_inc(sem("g_tf"), 1)
                elif s == 19:
                    act.wait_ge(*upto("g_wt_ps", h + 1))
                    if h:
                        act.wait_ge(*upto("g_v_ps", 4 * h))
                    A(g_wt[:, :, :], quad(side[3]), ACT.Copy, scale=-1.0).then_inc(sem("g_wt"), 1)
                elif 20 <= s < 28 and s % 2 == 0:
                    c = (s - 20) // 2
                    act.wait_ge(*upto("g_v_ps", 4 * h + c + 1))
                    if 4 * h + c >= 2:
                        act.wait_ge(*upto("g_o_ps", 4 * h + c - 1))
                    A(vnew[:, c % 2, :], side[c % 2][:, 0:P], ACT.Copy).then_inc(sem("g_vcopy"), 1)
                elif s == 27:
                    act.wait_ge(*upto("g_state", 4 * h + 4))
                    act.dma_start(O["p_gdn"][h], state_a[:, 1, :]).then_inc(sem("out_pgdn"), 16)
                elif s == 28:
                    act.wait_ge(*upto("g_o_ps", 4 * h + 4))
                    A(g_e1[:, :, :], quad(side[2]), ACT.Square).then_inc(sem("g_ysq"), 1)
                    act.wait_ge(*upto("g_y_ss", h + 1))
                    A(g_s[:, 5, 0:4], g_s[:, 5, 0:4], ACT.Ln, scale=1.0 / P, bias=eps[:, 0:1]).then_inc(sem("g_yln"), 1)
                    act.wait_ge(*upto("g_yln", h + 1))
                    A(g_s[:, 5, 4:8], g_s[:, 5, 0:4], ACT.Exp, scale=-0.5).then_inc(sem("g_yr"), 1)
                elif s == 29:
                    act.wait_ge(*upto("g_y_turned", h + 1))
                    if h == 0:
                        act.wait_ge(*upto("s_inter", NC - 1))
                    A(quad(y_raw[:, h, DB:NT]), quad(side[3]), ACT.Copy).then_inc(sem("g_y_copied"), 1)
            elif k == "att":
                h, c, s = it[1:]
                i = NC * h + c
                if s == 0:
                    if i == 0:
                        act.wait_ge(*upto("g_y_turned", GDN_H))
                        act.wait_ge(*upto("out_pgdn", 16 * GDN_H))
                        for j in range(4):
                            state_load(j)
                    act.wait_ge(*upto("a_nmax", i + 1))
                    if i >= 2:
                        act.wait_ge(*upto("a_turned", i - 1))
                    A(att_p[:, i % 2, :], side[i % 2][:, 0:MEM_T], ACT.Exp, scale=P ** -0.5, bias=att_s[:, 1, i:i + 1],
                      accum_out=att_s[:, 2, i:i + 1]).then_inc(sem("a_exp"), 1)
                elif s == 1:
                    act.wait_ge(*upto("a_turned", i + 1))
                    if i >= 2:
                        act.wait_ge(*upto("a_y_ps", i - 1))
                    A(att_pt[:, i % 2, :, :].rearrange("p m t -> p (m t)"), side[2][:, 256 * (i % 2):256 * (i % 2) + 256], ACT.Copy).then_inc(sem("a_pt"), 1)
            elif k == "atty":
                h = it[1]
                if it[2] == 0:
                    act.wait_ge(*upto("a_y_div", h + 1))
                    if h:
                        act.wait_ge(*upto("a_y_ss", h))
                    A(a_sq[:, :, :], a_y[:, :, :], ACT.Square).then_inc(sem("a_ysq"), 1)
                    act.wait_ge(*upto("a_y_ss", h + 1))
                    A(att_s[:, 5, 4 * h:4 * h + 4], att_s[:, 4, 4 * h:4 * h + 4], ACT.Ln, scale=1.0 / P, bias=eps[:, 0:1]).then_inc(sem("a_yln"), 1)
                    act.wait_ge(*upto("a_yln", h + 1))
                    A(att_s[:, 6, 4 * h:4 * h + 4], att_s[:, 5, 4 * h:4 * h + 4], ACT.Exp, scale=-0.5).then_inc(sem("a_yr"), 1)
                else:
                    act.wait_ge(*upto("a_y_turned", h + 1))
                    A(quad(y_raw[:, 16 + h, DB:NT]), quad(side[3]), ACT.Copy).then_inc(sem("a_y_copied"), 1)
            elif k == "decssd0":
                act.wait_ge(*upto("g_y_copied", GDN_H))
                act.wait_ge(*upto("g_y_turned", GDN_H))
                act.wait_ge(*upto("a_y_turned", MEM_H))
                act.wait_ge(*upto("d_k_ps", 1))
                A(d_k[:, 0:2, :, :].rearrange("p v t b -> p (v t b)"), side[0][:, 0:P], ACT.Copy).then_inc(sem("d_k"), 1)
            elif k == "decbc":
                g = it[1]
                act.wait_ge(*upto("d_bb_ps", g + 1))
                if g:
                    act.wait_ge(*upto("d_outer1", 4))
                A(d_bb[:, 0, :, :].rearrange("p b n -> p (b n)"), ps[:, 4:6, :].rearrange("p b q -> p (b q)"), ACT.Copy).then_inc(sem("d_bb"), 1)
                if g:
                    act.wait_ge(*upto("d_ymul", 4))
                A(d_bb[:, 1, :, :].rearrange("p b n -> p (b n)"), ps[:, 6:8, :].rearrange("p b q -> p (b q)"), ACT.Copy).then_inc(sem("d_bb"), 1)
            elif k == "decssd":
                state_step(it[1])
            elif k == "decgdn0":
                A(d_sq[:, 0, :, :], dec[:, N_SSD_T:N_SSD_T + GDN_H, :], ACT.Square).then_inc(sem("d_sq"), 1)
                A(d_sq[:, 1, :, :], dec[:, N_SSD_T + GDN_H:N_SSD_T + 2 * GDN_H, :], ACT.Square).then_inc(sem("d_sq"), 1)
                act.wait_ge(*upto("d_ss_ps", 1))
                ln = d_ln[:, :, :, :].rearrange("p a h b -> p (a h b)")
                A(ln, side[0][:, 0:P], ACT.Ln, bias=eps[:, 0:1]).then_inc(sem("d_ln"), 1)
                act.wait_ge(*upto("d_ln", 1))
                A(ln, ln, ACT.Exp, scale=-0.5).then_inc(sem("d_ln"), 1)
                A(d_g[:, :, :, :].rearrange("p a h b -> p (a h b)"), side[0][:, P:P + 192], ACT.Copy).then_inc(sem("d_g"), 1)
            elif k == "decgdn" and it[2] == 0:
                state_step(8 + it[1])
            elif k == "decattk":
                state_step(16 + it[1])
            elif k == "decatts":
                act.wait_ge(*upto("d_nmax", 1))
                A(d_p[0:pairs, :, :].rearrange("p m j -> p (m j)"), side[0][0:pairs, 0:MEM_T], ACT.Exp, scale=P ** -0.5, bias=d_sv[0:pairs, 1:2],
                  accum_out=d_sv[0:pairs, 2:3]).then_inc(sem("d_pexp"), 1)
            elif k == "decattv":
                state_step(24 + it[1])
            elif k == "decatty" and it[1] == 0:
                act.wait_ge(*upto("d_pv", DB))
                A(d_p[0:pairs, 0, :], side[3][0:pairs, 0:P], ACT.Copy).then_inc(sem("d_yt"), 1)
            elif k == "decatty":
                act.wait_ge(*upto("d_yt_ps", 1))
                A(y_dec[:, 16:20, :], side[2][:, 0:pairs].rearrange("p (b h) -> p h b", h=MEM_H), ACT.Copy).then_inc(sem("y_dec_mem"), 1)
            elif k == "decnorm":
                act.wait_ge(*upto("y_dec_mem", 1))
                act.wait_ge(*upto("y_dec_ssd", 8))
                act.wait_ge(*upto("y_dec_gdn", GDN_H))
                A(d_n[:, 0, :, :], y_dec[:, :, :], ACT.Square).then_inc(sem("d_ysq"), 1)
                act.wait_ge(*upto("d_yss", 1))
                n1 = d_n[:, 1, :, :].rearrange("p e b -> p (e b)")
                A(n1[:, 0:64], side[0][:, 0:64], ACT.Ln, scale=1.0 / SSD_P, bias=eps[:, 0:1]).then_inc(sem("d_yln"), 1)
                A(n1[:, 64:160], side[0][:, 64:160], ACT.Ln, scale=1.0 / P, bias=eps[:, 0:1]).then_inc(sem("d_yln"), 1)
                act.wait_ge(*upto("d_yln", 2))
                A(n1, n1, ACT.Exp, scale=-0.5).then_inc(sem("d_yr"), 1)
            elif k == "yhi":
                e = it[1]
                if e == 0:
                    for j in range(4):
                        act.wait_ge(sem(f"out_st{j}"), 16 * 4)
                if e in (0, 8, 16):
                    act.wait_ge(*upto("dec_gated", 2 * (e // 8 + 1)))
                act.wait_ge(*upto("z_gated", e + 1))
                A(y_hi[:, SLOT[e], :], y_raw[:, SLOT[e], :], ACT.Copy).then_inc(sem("y_hi_done"), 1)
            elif k == "out" and unit_of(it)[1] in (0, 3):
                g, b = unit_of(it)
                split_hi(g + 1, 0 if b == 0 else 1)
            elif k == "fin" and it[2] == 1:
                n = it[1]
                act.wait_ge(*upto("fin_added", n + 1))
                if n >= 2:
                    act.wait_ge(*upto("fin_acc", n - 1))
                A(fin_sq[:, n % 2, :], fin[:, n, :], ACT.Square).then_inc(sem("fin_sq"), 1)
            elif k == "fin" and it[2] == 2:
                n = it[1]
                act.wait_ge(*upto("fin_sq", n + 1))
                if n == 0:
                    act.wait_ge(*upto("fin_w_in", 16))
                A(fin[:, n, :], fin[:, n, :], ACT.Copy, scale=fin_w[:, n:n + 1]).then_inc(sem("fin_weighted"), 1)
            elif k == "final":
                act.wait_ge(*upto("fin_ss", 1))
                A(halves(fin_r[:, :]), ps[:, 4:6, 0:HALF], ACT.Ln, scale=1.0 / D, bias=eps[:, 0:1]).then_inc(sem("fin_ln"), 1)
                act.wait_ge(*upto("fin_ln", 1))
                A(fin_r[:, :], fin_r[:, :], ACT.Exp, scale=-0.5).then_inc(sem("fin_r"), 1)

    @block.vector
    def _(dve):
        V = nc.vector

        def split_lo(g, piece):
            if g >= N_UNITS or g in pool_units:
                return
            dve.wait_ge(*upto("w_hi_done", 2 * g + piece + 1))
            s = slice(512 * piece, 512 * piece + 512)
            V.tensor_tensor(w_lo[:, g % 2, s], raw[:, g % NRAW, s], w_hi[:, g % 2, s].bitcast(F32), ALU.subtract).then_inc(sem("w_lo_done"), 1)

        def x_lo(kk):
            dve.wait_ge(*upto("x_hi", kk + 1))
            V.tensor_tensor(h_lo[:, kk, :], x_w[:, kk % 2, :], h_hi[:, kk, :].bitcast(F32), ALU.subtract).then_inc(sem("x_lo_v"), 1)

        def ssd_scores(c, qd):
            i = 4 * c + qd
            dve.wait_ge(*upto("s_exp", i + 1))
            if qd == 0:
                dve.wait_ge(*upto("s_bcopy", 2 * (c + 1)))
            V.tensor_tensor(s_l[:, i % 2, :, :], s_l[:, i % 2, :, :], across(s_cb[:, qd // 2, :], 4), ALU.mult).then_inc(sem("s_scores"), 1)

        for it in items:
            k = it[0]
            if k == "const":
                V.memset(eps[:, 0:1], EPS).then_inc(sem("eps_set"), 1)
                V.memset(eps[:, 1:2], 1.0).then_inc(sem("eps_set"), 1)
            elif k == "xsq" and it[1] % 2 == 1:
                kk = it[1]
                dve.wait_ge(*upto("x_sq", kk + 1))
                pair = x_sq[kk // 2 % 2]
                V.tensor_tensor(pair[:, 0, :], pair[:, 0, :], pair[:, 1, :], ALU.add).then_inc(sem("x_sq_sum"), 1)
            elif k == "xrstd":
                dve.wait_ge(*upto("ident_in", 16))
                V.tensor_copy(ident_r[:, :], ident_f).then_inc(sem("ident_r"), 1)
                split_lo(0, 0)
                split_lo(0, 1)
                split_lo(1, 0)
                split_lo(1, 1)
                dve.wait_ge(*upto("vecs_in", 16))
            elif k == "xh":
                kk = it[1]
                dve.wait_ge(*upto("rstd", 1))
                if kk >= 2:
                    dve.wait_ge(*upto("x_hi", kk - 1))
                    dve.wait_ge(*upto("x_lo_g", (kk - 1) // 2 + (kk - 1) % 2) if kk % 2 == 0 else upto("x_lo_v", kk // 2))
                V.scalar_tensor_tensor(x_w[:, kk % 2, :], x_t[:, kk, :], norm_w[:, kk:kk + 1], x_rstd, ALU.mult, ALU.mult).then_inc(sem("x_w"), 1)
                if kk >= 2 and kk % 2 == 0:
                    x_lo(kk - 1)
            elif k == "setup":
                x_lo(KT - 1)
                dve.wait_ge(*upto("wsm_in", 16))
                V.tensor_copy(wsm_hi[:, :, :], wsm_raw[:, :, :]).then_inc(sem("wsm_split"), 1)
                dve.wait_ge(*upto("wsm_split", 1))
                V.tensor_tensor(wsm_lo[:, :, :], wsm_raw[:, :, :], wsm_hi[:, :, :].bitcast(F32), ALU.subtract).then_inc(sem("wsm_split"), 1)
                dve.wait_ge(*upto("hist_in", 16))
                for j in range(3):
                    dst = hist[:, :, :] if j == 0 else hist_tmp[:, :, :]
                    if j >= 1:
                        dve.wait_ge(*upto("hist_step", 2 * j - 1))
                    V.tensor_tensor(dst, hist3[:, :, :, j], along(conv_w[:, :, j], DB), ALU.mult).then_inc(sem("hist_step"), 1)
                    if j >= 1:
                        dve.wait_ge(*upto("hist_step", 2 * j))
                        V.tensor_tensor(hist[:, :, :], hist[:, :, :], hist_tmp[:, :, :], ALU.add).then_inc(sem("hist_step"), 1)
            elif k == "mh":
                kk = it[1]
                dve.wait_ge(*upto("rstd", 2))
                if kk >= 2:
                    dve.wait_ge(*upto("m_hi", kk - 1))
                    dve.wait_ge(*upto("m_lo", kk - 1))
                src = mem_t[:, kk, :] if kk < 8 else mem_t2[:, kk - 8, :]
                V.scalar_tensor_tensor(m_w[:, kk % 2, :], src, mem_norm_w[:, kk:kk + 1], m_rstd[:, :], ALU.mult, ALU.mult).then_inc(sem("m_w"), 1)
            elif k == "kv":
                split_lo(ring[it] + 1, 0)
                split_lo(ring[it] + 1, 1)
            elif k == "kvout":
                dve.wait_ge(*upto("unit_used", kv_units))
                for m in range(2):
                    V.tensor_copy(mv[:, m, :], side[2 + m]).then_inc(sem("mv_done"), 1)
            elif k == "smallturn":
                dve.wait_ge(*upto("small_ps", 1))
                V.tensor_copy(halves(sm_t[0:SM, :]), ps[0:SM, 4:6, 0:HALF]).then_inc(sem("small_copied"), 1)
            elif k == "smallpost":
                dve.wait_ge(*upto("small_done", 1))
                x, b_cols = sp_t[4], slice(SSD_H, SSD_H + GDN_H)
                V.tensor_tensor(x, side[3][:, 0:5 * SM].rearrange("p (t s) -> p t s", t=5), across(sm_bias, 5), ALU.add).then_inc(sem("small_step"), 1)
                dve.wait_ge(*upto("small_step", 1))
                V.tensor_scalar(x[:, :, b_cols], x[:, :, b_cols], -1.0, None, ALU.mult).then_inc(sem("small_step"), 1)
                dve.wait_ge(*upto("small_step", 2))
                V.tensor_scalar(sp_t[3], x, 0.0, None, ALU.max).then_inc(sem("small_step"), 1)
                dve.wait_ge(*upto("small_step", 3))
                V.scalar_tensor_tensor(sp_t[0], sp_t[3], 2.0, x, ALU.mult, ALU.subtract).then_inc(sem("small_step"), 1)
                dve.wait_ge(*upto("small_step", 4))
                V.tensor_scalar(sp_t[5], x, 0.0, None, ALU.max).then_inc(sem("sp_abs"), 1)
            elif k == "smallpost2":
                dve.wait_ge(*upto("sp_abs", 1))
                dve.wait_ge(*upto("sp_ln", 1))
                e = sp_t[1]
                V.tensor_scalar(sp_t[0], e, -0.25, 1.0 / 3, ALU.mult, ALU.add).then_inc(sem("small_step"), 1)
                dve.wait_ge(*upto("small_step", 5))
                V.tensor_tensor(sp_t[0], sp_t[0], e, ALU.mult).then_inc(sem("small_step"), 1)
                dve.wait_ge(*upto("small_step", 6))
                V.tensor_scalar(sp_t[0], sp_t[0], -1.0, 0.5, ALU.mult, ALU.add).then_inc(sem("small_step"), 1)
                dve.wait_ge(*upto("small_step", 7))
                V.tensor_tensor(sp_t[0], sp_t[0], e, ALU.mult).then_inc(sem("small_step"), 1)
                dve.wait_ge(*upto("small_step", 8))
                V.tensor_scalar(sp_t[0], sp_t[0], -1.0, 1.0, ALU.mult, ALU.add).then_inc(sem("small_step"), 1)
                dve.wait_ge(*upto("small_step", 9))
                V.tensor_tensor(sp_t[0], sp_t[0], e, ALU.mult).then_inc(sem("small_step"), 1)
                dve.wait_ge(*upto("small_step", 10))
                V.tensor_tensor(sp_t[0], sp_t[0], sp_t[2], ALU.subtract).then_inc(sem("small_step"), 1)
                dve.wait_ge(*upto("small_step", 11))
                V.tensor_scalar(sp_t[4], e, 0.03, None, ALU.is_lt).then_inc(sem("small_step"), 1)
                dve.wait_ge(*upto("small_step", 12))
                V.tensor_tensor(sp_t[0], sp_t[0], sp_t[4], ALU.mult).then_inc(sem("small_step"), 1)
                dve.wait_ge(*upto("small_step", 13))
                V.tensor_tensor(sp_t[0], sp_t[0], sp_t[2], ALU.add).then_inc(sem("small_step"), 1)
                dve.wait_ge(*upto("small_step", 14))
                V.tensor_tensor(sp[:, :, :], sp_t[0], sp_t[5], ALU.add).then_inc(sem("sp_done"), 1)
                dve.wait_ge(*upto("sp_done", 1))
                dve.wait_ge(*upto("a_done", 1))
                V.scalar_tensor_tensor(da[:, :, :], sp[:, :, :], -1.0, across(sm_a, 5), ALU.mult, ALU.mult).then_inc(sem("da_done"), 1)
            elif k == "smallend":
                b_cols = slice(SSD_H, SSD_H + GDN_H)
                dve.wait_ge(*upto("cum_done", 1))
                V.tensor_copy(cum[:, :, :].rearrange("p c h -> p (c h)"), side[2][:, 0:P]).then_inc(sem("cum_copied"), 1)
                V.tensor_copy(tot[:, :, :].rearrange("p c h -> p (c h)"), side[2][:, P:2 * P]).then_inc(sem("cum_copied"), 1)
                dve.wait_ge(*upto("cum_copied", 2))
                V.tensor_tensor(w_end[:, :, :], tot[:, :, 0:SSD_H], cum[:, :, 0:SSD_H], ALU.subtract).then_inc(sem("w_end_diff"), 1)
                gcum = cum[:, :, SSD_H + GDN_H:SM]
                V.tensor_tensor(row_a0[:, :, :], gcum, sp[:, 0:NC, b_cols], ALU.subtract).then_inc(sem("row0"), 1)
                V.tensor_scalar(row_q0[:, :, :], gcum, -0.5 * float(np.log(P)), None, ALU.add).then_inc(sem("row0"), 1)
                dve.wait_ge(*upto("w_end_exp", 1))
                V.tensor_tensor(w_end[:, :, :], w_end[:, :, :], sp[:, 0:NC, 0:SSD_H], ALU.mult).then_inc(sem("w_end_done"), 1)
                dve.wait_ge(*upto("masks_in", 16))
                V.tensor_copy(masks[:, :, :], masks_f[:, :, :]).then_inc(sem("masks_done"), 1)
            elif k == "proj" and it[2] % 8 in (2, 5):
                g, b = unit_of(it)
                if g:
                    split_lo(g + 1, 0 if b == 2 else 1)
            elif k == "post":
                n, s = it[1], it[2]
                kind, i, _ = TILES[n]
                if kind in ("ssd", "gdn") and 1 <= s <= 4:
                    ci, sq = conv_index(n), conv_at[n]
                    u, a = conv_u[:, sq % 2, :], conv_a[:, sq % 2, :]
                    if s == 1:
                        dve.wait_ge(*upto("conv_u", sq + 1))
                        dve.wait_ge(*upto("tile_read", n + 1))
                    else:
                        dve.wait_ge(*upto("tap_done", 4 * sq + s - 1))
                    if s < 4:
                        V.scalar_tensor_tensor(a[:, DB + s:NT], u[:, DB:NT - s], conv_w[:, ci, 3 - s:4 - s], a[:, DB + s:NT], ALU.mult, ALU.add).then_inc(sem("tap_done"), 1)
                    else:
                        if sq == 0:
                            dve.wait_ge(*upto("hist_step", 5))
                        V.tensor_tensor(a[:, 0:DB], a[:, 0:DB], hist[:, ci, :], ALU.add).then_inc(sem("tap_done"), 1)
                elif kind == "z" and s == 2:
                    zi, e = z_at[n], TILES[n][1]
                    dve.wait_ge(*upto("tile_read", n + 1))
                    if e == 0:
                        dve.wait_ge(*upto("s_y_copied", NC))
                    if e == 8:
                        dve.wait_ge(*upto("g_y_copied", GDN_H))
                    if e == 16:
                        dve.wait_ge(*upto("a_y_copied", MEM_H))
                    y = y_raw[:, SLOT[e], DB:NT]
                    V.scalar_tensor_tensor(y, conv_a[:, zi % 2, DB:NT], mix_w[:, e:e + 1], y, ALU.mult, ALU.mult).then_inc(sem("z_gated"), 1)
            elif k == "ssd":
                c, s = it[1], it[2]
                y2 = heads(s_y[:, c % 2, :])
                if s == 0:
                    dve.wait_ge(*upto("s_turned", c + 1))
                    x = heads(ps[:, 4:6, :])
                    if c == 0:
                        dve.wait_ge(*upto("w_end_done", 1))
                        dve.wait_ge(*upto("unit_used", kv_units))
                    else:
                        dve.wait_ge(*upto("s_stateps", c))
                        dve.wait_ge(*upto("s_intra", 4 * c))
                    if c >= 2:
                        dve.wait_ge(*upto("s_y_turned", c - 1))
                    V.tensor_tensor(heads(s_xdt[:, :]), x, along(sp[:, c, 0:SSD_H], SSD_P), ALU.mult).then_inc(sem("s_x_read"), 1)
                    V.tensor_tensor(y2, x, along(sm_d, SSD_P), ALU.mult).then_inc(sem("s_x_read"), 1)
                    V.tensor_tensor(heads(s_xw[:, :]), x, along(w_end[:, c, :], SSD_P), ALU.mult).then_inc(sem("s_x_read"), 1)
                elif s == 1 and c > 0:
                    dve.wait_ge(*upto("s_inter", c))
                    dve.wait_ge(*upto("s_red", c))
                    V.tensor_tensor(heads(s_tmp[:, :]), heads(ps[:, 4:6, :]), along(e_cum[:, c, :], SSD_P), ALU.mult).then_inc(sem("s_inter_read"), 1)
                    dve.wait_ge(*upto("s_inter_read", c))
                    dve.wait_ge(*upto("s_x_read", 3 * (c + 1)))
                    V.tensor_tensor(s_y[:, c % 2, :], s_y[:, c % 2, :], s_tmp[:, :], ALU.add).then_inc(sem("s_inter_add"), 1)
                if 3 <= s <= 6:
                    ssd_scores(c, s - 3)
                if 2 <= s <= 5:
                    i = 4 * c + s - 2
                    dve.wait_ge(*upto("s_rows", i + 1))
                    if i >= 2:
                        dve.wait_ge(*upto("s_intra", i - 1))
                    V.tensor_tensor(s_l[:, i % 2, :, :], quad(side[3]), along(cum[:, c, 4 * (s - 2):4 * (s - 2) + 4], P), ALU.subtract).then_inc(sem("s_sub"), 1)
                if s == 6:
                    dve.wait_ge(*upto("s_intra", 4 * (c + 1)))
                    dve.wait_ge(*upto("s_x_read", 3 * (c + 1)))
                    if c:
                        dve.wait_ge(*upto("s_inter_add", c))
                    V.tensor_tensor(s_y[:, c % 2, :], ps[:, 4:6, :].rearrange("p b q -> p (b q)"), s_y[:, c % 2, :], ALU.add).then_inc(sem("s_intra_read"), 1)
                    dve.wait_ge(*upto("s_intra_read", c + 1))
                    dve.wait_ge(*upto("s_stateps", c + 1))
                    dst = ps[:, 6:8, :].rearrange("p b q -> p (b q)")
                    if c == 0:
                        V.tensor_copy(s_state[:, :], dst).then_inc(sem("s_state_new"), 1)
                    else:
                        V.tensor_tensor(heads(s_state[:, :]), heads(s_state[:, :]), along(e_tot[:, c, 0:SSD_H], SSD_P), ALU.mult).then_inc(sem("s_decayed"), 1)
                        dve.wait_ge(*upto("s_decayed", c))
                        V.tensor_tensor(s_state[:, :], dst, s_state[:, :], ALU.add).then_inc(sem("s_state_new"), 1)
                if s == 7:
                    dve.wait_ge(*upto("s_ysq", c + 1))
                    if c:
                        dve.wait_ge(*upto("s_yln", c))
                    V.reduce_sum(s_red[:, 0, :], heads(s_tmp[:, :]), axis=AX).then_inc(sem("s_red"), 1)
                if s == 8:
                    dve.wait_ge(*upto("s_yr", c + 1))
                    V.tensor_tensor(y2, y2, along(s_red[:, 2, :], SSD_P), ALU.mult).then_inc(sem("s_y_normed"), 1)
            elif k == "gdn":
                h, s = it[1], it[2]
                gc = SSD_H + GDN_H + h
                if s == 0:
                    dve.wait_ge(*upto("g_ln", h + 1))
                    lq, lk = g_s[:, 0, 0:4], g_s[:, 0, 4:8]
                    if h:
                        dve.wait_ge(*upto("g_ea", h))
                        dve.wait_ge(*upto("g_rows", h))
                    V.scalar_tensor_tensor(g_row[:, 0, :], lk, -0.5, row_a0[:, :, h], ALU.mult, ALU.add).then_inc(sem("g_rowx"), 1)
                    V.scalar_tensor_tensor(g_row[:, 1, :], lq, -0.5, row_q0[:, :, h], ALU.mult, ALU.add).then_inc(sem("g_row"), 1)
                    V.scalar_tensor_tensor(g_s[:, 2, 0:4], lk, -0.5, cum[:, :, gc], ALU.mult, ALU.subtract).then_inc(sem("g_col"), 1)
                    dve.wait_ge(*upto("g_col", h + 1))
                    V.tensor_tensor(g_s[:, 4, 0:4], g_s[:, 2, 0:4], tot[:, :, gc], ALU.add).then_inc(sem("g_colt"), 1)
                    if h:
                        dve.wait_ge(*upto("g_v_ps", 4 * h))
                        dve.wait_ge(*upto("g_o_ps", 4 * h))
                    V.tensor_tensor(g_r1[:, :, :], quad(side[1]), along(beta[:, 0:NC, h], P), ALU.mult).then_inc(sem("g_scaled"), 1)
                    dve.wait_ge(*upto("g_ea", h + 1))
                    V.tensor_tensor(g_r2[:, :, :], quad(side[0]), along(g_s[:, 3, 0:4], P), ALU.mult).then_inc(sem("g_scaled"), 1)
                    dve.wait_ge(*upto("g_ke", h + 1))
                    V.tensor_tensor(g_kend[:, :, :], quad(side[0]), along(g_s[:, 4, 0:4], P), ALU.mult).then_inc(sem("g_scaled"), 1)
                elif s == 1:
                    dve.wait_ge(*upto("g_rows", h + 1))
                    V.tensor_tensor(g_e1[:, :, :], quad(side[2]), along(g_s[:, 2, 0:4], P), ALU.add).then_inc(sem("g_sub"), 1)
                    V.tensor_tensor(g_e2[:, :, :], quad(side[3]), along(g_s[:, 2, 0:4], P), ALU.add).then_inc(sem("g_sub"), 1)
                    dve.wait_ge(*upto("g_qrow", h + 1))
                    V.tensor_tensor(g_qg[:, :, :], g_qg[:, :, :], quad(gconv[:, 0, DB:NT]), ALU.mult).then_inc(sem("g_qg"), 1)
                elif s == 2:
                    dve.wait_ge(*upto("g_gram", h + 1))
                    dve.wait_ge(*upto("g_exp", 2 * h + 1))
                    V.scalar_tensor_tensor(flat4(g_natf), side[0], -1.0, flat4(g_e1), ALU.mult, ALU.mult).then_inc(sem("g_nat"), 1)
                    dve.wait_ge(*upto("g_exp", 2 * h + 2))
                    V.tensor_tensor(g_attn[:, :, :], quad(side[1]), g_e2[:, :, :], ALU.mult).then_inc(sem("g_attn"), 1)
                elif s == 3:
                    dve.wait_ge(*upto("g_natm", 7 * h + 1))
                    V.tensor_tensor(g_tt[:, :, :], g_natm[0][:, :, :].bitcast(F32), across(ident, NC), ALU.add).then_inc(sem("g_tt0"), 1)
                    dve.wait_ge(*upto("g_t0_ps", h + 1))
                    V.tensor_tensor(g_t[:, :, :], quad(side[0]), across(ident, NC), ALU.add).then_inc(sem("g_t_new"), 1)
                elif 4 <= s < 16 and s % 2 == 0:
                    level = (s - 2) // 2
                    dve.wait_ge(*upto("g_at", 6 * h + level))
                    V.tensor_tensor(g_p[:, :, :], quad(side[1]), across(ident, NC), ALU.add).then_inc(sem("g_p"), 1)
                elif 4 <= s < 14:
                    level = (s - 3) // 2
                    dve.wait_ge(*upto("g_tat", 6 * h + level))
                    V.tensor_copy(g_t[:, :, :], quad(side[2])).then_inc(sem("g_t_new"), 1)
                elif s == 17:
                    dve.wait_ge(*upto("g_res_ps", h + 1))
                    if h:
                        dve.wait_ge(*upto("g_y_turned", h))
                    V.tensor_tensor(g_res[:, :, :], quad(side[1]), g_tf[:, :, :], ALU.subtract).then_inc(sem("g_resx"), 1)
                    dve.wait_ge(*upto("g_resx", h + 1))
                    V.tensor_tensor(g_res[:, :, :], g_res[:, :, :], across(ident, NC), ALU.add).then_inc(sem("g_res"), 1)
                elif s == 18:
                    dve.wait_ge(*upto("g_fix_ps", h + 1))
                    V.tensor_tensor(g_ttf[:, :, :], quad(side[2]), g_tt[:, :, :].bitcast(F32), ALU.add).then_inc(sem("g_ttf"), 1)
                elif 20 <= s < 28 and s % 2 == 1:
                    c = (s - 21) // 2
                    dve.wait_ge(*upto("g_o_ps", 4 * h + c + 1))
                    if c == 0:
                        V.tensor_copy(state_a[:, 0, :], side[3][:, 0:P]).then_inc(sem("g_state"), 1)
                    else:
                        if c == 1 and h:
                            dve.wait_ge(*upto("out_pgdn", 16 * h))
                        dve.wait_ge(*upto("g_state", 4 * h + c))
                        V.scalar_tensor_tensor(state_a[:, c % 2, :], state_a[:, (c - 1) % 2, :], e_tot[:, c, gc:gc + 1], side[3][:, 0:P], ALU.mult, ALU.add).then_inc(sem("g_state"), 1)
                elif s == 28:
                    dve.wait_ge(*upto("g_ysq", h + 1))
                    if h:
                        dve.wait_ge(*upto("g_yr", h))
                    V.reduce_sum(g_s[:, 5, 0:4], g_e1[:, :, :], axis=AX).then_inc(sem("g_y_ss"), 1)
                    dve.wait_ge(*upto("g_yr", h + 1))
                    dve.wait_ge(*upto("g_fix_ps", h + 1))
                    V.tensor_tensor(g_res[:, :, :], quad(side[2]), along(g_s[:, 5, 4:8], P), ALU.mult).then_inc(sem("g_y_scaled"), 1)
            elif k == "att" and it[3] == 0:
                h, c, s = it[1:]
                i = NC * h + c
                dve.wait_ge(*upto("a_scores", i + 1))
                V.reduce_max(att_s[:, 0, i:i + 1], side[i % 2][:, 0:MEM_T], axis=AX).then_inc(sem("a_max"), 1)
                dve.wait_ge(*upto("a_max", i + 1))
                V.tensor_scalar(att_s[:, 1, i:i + 1], att_s[:, 0, i:i + 1], -(P ** -0.5), None, ALU.mult).then_inc(sem("a_nmax"), 1)
            elif k == "atty" and it[2] == 0:
                h = it[1]
                cols = slice(4 * h, 4 * h + 4)
                dve.wait_ge(*upto("a_exp", NC * (h + 1)))
                V.reciprocal(att_s[:, 3, cols], att_s[:, 2, cols]).then_inc(sem("a_rec"), 1)
                dve.wait_ge(*upto("a_rec", h + 1))
                dve.wait_ge(*upto("a_y_ps", NC * (h + 1)))
                if h:
                    dve.wait_ge(*upto("a_y_turned", h))
                else:
                    dve.wait_ge(*upto("g_y_turned", GDN_H))
                V.tensor_tensor(a_y[:, :, :], quad(side[3]), along(att_s[:, 3, cols], P), ALU.mult).then_inc(sem("a_y_div"), 1)
                dve.wait_ge(*upto("a_ysq", h + 1))
                V.reduce_sum(att_s[:, 4, cols], a_sq[:, :, :], axis=AX).then_inc(sem("a_y_ss"), 1)
                dve.wait_ge(*upto("a_yr", h + 1))
                V.tensor_tensor(a_y[:, :, :], a_y[:, :, :], along(att_s[:, 6, cols], P), ALU.mult).then_inc(sem("a_y_scaled"), 1)
            elif k == "decssd0":
                dve.wait_ge(*upto("g_y_turned", GDN_H))
                dve.wait_ge(*upto("a_y_turned", MEM_H))
                dve.wait_ge(*upto("out_pgdn", 16 * GDN_H))
                dve.wait_ge(*upto("e_da_done", 1))
                for dst, src in ((d_tmp, sp[0:DB, 4, 0:SSD_H]), (d_tmp2, e_da[0:DB, 0:SSD_H])):
                    V.tensor_copy(heads(dst[0:DB, :, :]), along(src, SSD_P)).then_inc(sem("d_wide"), 1)
                dve.wait_ge(*upto("d_k", 1))
                V.tensor_tensor(d_k[:, 2, :, :], d_k[:, 0, :, :], dec[:, 0:8, :], ALU.mult).then_inc(sem("d_dtx"), 1)
            elif k == "decssdy":
                i = it[1]
                st = d_st[:, i % 4, :, :]
                dve.wait_ge(*upto("d_decayed", i + 1))
                dve.wait_ge(*upto("d_outer1", i + 1))
                V.tensor_tensor(st, st, d_tmp[:, :, :], ALU.add).then_inc(sem("d_new"), 1)
                dve.wait_ge(*upto("d_new", i + 1))
                if i % 4 == 0:
                    dve.wait_ge(*upto("d_bb", 2 * (i // 4 + 1)))
                if i:
                    dve.wait_ge(*upto("d_yred", i))
                V.tensor_tensor(d_tmp2[:, :, :], st, d_bb[:, 1, :, :], ALU.mult).then_inc(sem("d_ymul"), 1)
                dve.wait_ge(*upto("d_ymul", i + 1))
                V.reduce_sum(y_dec[:, i, :], d_tmp2[:, :, :], axis=AX).then_inc(sem("d_yred"), 1)
                dve.wait_ge(*upto("d_yred", i + 1))
                V.scalar_tensor_tensor(y_dec[:, i, :], dec[:, i, :], d_lay[:, i:i + 1], y_dec[:, i, :], ALU.mult, ALU.add).then_inc(sem("y_dec_ssd"), 1)
            elif k == "decgdn0":
                q, kk_ = dec[:, N_SSD_T:N_SSD_T + GDN_H, :], dec[:, N_SSD_T + GDN_H:N_SSD_T + 2 * GDN_H, :]
                V.tensor_tensor(d_sq[:, 2, :, :], q, kk_, ALU.mult).then_inc(sem("d_sqv"), 1)
                for j, val in enumerate((beta[0:DB, 4, :], e_da[0:DB, SSD_H + GDN_H:SM])):
                    V.tensor_tensor(d_sel[0:DB, j, :, :], across(ident[0:DB, 0:DB], GDN_H), along(val, DB), ALU.mult).then_inc(sem("d_sel"), 1)
                dve.wait_ge(*upto("d_ln", 2))
                V.tensor_tensor(d_kq[:, :, :, 0], kk_, d_ln[:, 1, :, :], ALU.mult).then_inc(sem("d_kq"), 1)
                V.scalar_tensor_tensor(d_kq[:, :, :, 1], q, P ** -0.5, d_ln[:, 0, :, :], ALU.mult, ALU.mult).then_inc(sem("d_kq"), 1)
                dve.wait_ge(*upto("d_g", 1))
                V.scalar_tensor_tensor(d_g[:, 0, :, :], d_g[:, 0, :, :], P ** -0.5, d_ln[:, 0, :, :], ALU.mult, ALU.mult).then_inc(sem("d_qk"), 1)
                dve.wait_ge(*upto("d_qk", 1))
                V.tensor_tensor(d_g[:, 0, :, :], d_g[:, 0, :, :], d_ln[:, 1, :, :], ALU.mult).then_inc(sem("d_qk"), 1)
                dve.wait_ge(*upto("d_qk", 2))
                dve.wait_ge(*upto("sel_zero", 1))
                V.tensor_copy(q_sel[:, 0:pairs * pairs:pairs + 1].rearrange("p (b h) -> p h b", h=MEM_H), dec[:, NCONV:NCONV + MEM_H, :]).then_inc(sem("d_qsel"), 1)
            elif k == "decgdn" and it[2] == 0:
                h = it[1]
                ks = side[1][:, 0:2 * DB].rearrange("p (b j) -> p b j", j=2)
                qk, bt, eg = (d_g[:, j, h, :] for j in range(3))
                dve.wait_ge(*upto("d_ks", h + 1))
                if h:
                    dve.wait_ge(*upto("d_vb", h))
                V.tensor_tensor(d_v[:, 0, :], ks[:, :, 0], eg, ALU.mult).then_inc(sem("d_ks_read"), 1)
                V.tensor_tensor(d_v[:, 1, :], ks[:, :, 1], eg, ALU.mult).then_inc(sem("d_ks_read"), 1)
                dve.wait_ge(*upto("d_ks_read", 2 * h + 2))
                V.tensor_tensor(d_v[:, 0, :], dec[:, N_SSD_T + 2 * GDN_H + h, :], d_v[:, 0, :], ALU.subtract).then_inc(sem("d_vsub"), 1)
                dve.wait_ge(*upto("d_vsub", h + 1))
                V.tensor_tensor(d_v[:, 2, :], d_v[:, 0, :], bt, ALU.mult).then_inc(sem("d_vn"), 1)
                dve.wait_ge(*upto("d_vn", h + 1))
                V.tensor_tensor(d_v[:, 3, :], d_v[:, 2, :], qk, ALU.mult).then_inc(sem("d_vqk"), 1)
                dve.wait_ge(*upto("d_vqk", h + 1))
                V.tensor_tensor(y_dec[:, 8 + h, :], d_v[:, 3, :], d_v[:, 1, :], ALU.add).then_inc(sem("y_dec_gdn"), 1)
            elif k == "decgdn":
                h = it[1]
                st = d_st[:, h % 4, :, :]
                dve.wait_ge(*upto("d_vb", h + 1))
                if h == 0:
                    dve.wait_ge(*upto("d_new", 8))
                V.tensor_tensor(d_tmp[:, :, :], ps[:, 6:8, :].rearrange("p b (i t) -> p (b i) t", i=4), along(d_kq[:, h, :, 0], P), ALU.mult).then_inc(sem("d_outer"), 1)
                dve.wait_ge(*upto("d_outer", h + 1))
                dve.wait_ge(*upto("d_decayed", 8 + h + 1))
                V.tensor_tensor(st, st, d_tmp[:, :, :], ALU.add).then_inc(sem("d_new"), 1)
                dve.wait_ge(*upto("d_new", 8 + h + 1))
            elif k == "decatts":
                dve.wait_ge(*upto("d_sc_ps", DB))
                V.reduce_max(d_sv[0:pairs, 0:1], side[0][0:pairs, 0:MEM_T], axis=AX).then_inc(sem("d_max"), 1)
                dve.wait_ge(*upto("d_max", 1))
                V.tensor_scalar(d_sv[0:pairs, 1:2], d_sv[0:pairs, 0:1], -(P ** -0.5), None, ALU.mult).then_inc(sem("d_nmax"), 1)
                dve.wait_ge(*upto("d_pexp", 1))
                V.reciprocal(d_sv[0:pairs, 3:4], d_sv[0:pairs, 2:3]).then_inc(sem("d_rec"), 1)
                dve.wait_ge(*upto("d_rec", 1))
                V.tensor_scalar(d_p[0:pairs, :, :], d_p[0:pairs, :, :], d_sv[0:pairs, 3:4], None, ALU.mult).then_inc(sem("d_p"), 1)
            elif k == "decattp":
                dve.wait_ge(*upto("d_pt_ps", 1))
                dve.wait_ge(*upto("sel_zero", 2))
                V.tensor_copy(p_sel[:, :, 0:pairs * pairs:pairs + 1], side[2][:, 0:2 * pairs].rearrange("p (m i) -> p m i", m=2)).then_inc(sem("d_psel"), 1)
            elif k == "decnorm":
                dve.wait_ge(*upto("d_yr", 1))
                V.tensor_tensor(y_dec[:, :, :], y_dec[:, :, :], d_n[:, 1, :, :], ALU.mult).then_inc(sem("d_ynorm"), 1)
            elif k == "decgate":
                part = it[1]
                e0, e1 = ((0, 8), (8, 16), (16, 20))[part]
                dve.wait_ge(*upto("z_dec", e1))
                dve.wait_ge(*upto("d_ynorm", 1))
                V.tensor_tensor(y_dec[:, e0:e1, :], y_dec[:, e0:e1, :], z_dec[:, e0:e1, :], ALU.mult).then_inc(sem("dec_gated"), 1)
                dve.wait_ge(*upto("dec_gated", 2 * part + 1))
                V.tensor_tensor(y_raw[:, SLOT[e0]:SLOT[e0] + e1 - e0, 0:DB], y_dec[:, e0:e1, :], along(mix_w[:, e0:e1], DB), ALU.mult).then_inc(sem("dec_gated"), 1)
            elif k == "ylo" and it[1] % 2 == 1:
                e = it[1]
                if e == 1:
                    dve.wait_ge(*upto("unit_used", in_units))
                dve.wait_ge(*upto("y_hi_done", e + 1))
                V.tensor_tensor(y_lo[:, SLOT[e], :], y_raw[:, SLOT[e], :], y_hi[:, SLOT[e], :].bitcast(F32), ALU.subtract).then_inc(sem("y_lo_v"), 1)
            elif k == "out" and unit_of(it)[1] in (2, 5):
                g, b = unit_of(it)
                split_lo(g + 1, 0 if b == 2 else 1)
            elif k == "fin" and it[2] == 0:
                n = it[1]
                if (ET * (n + 1)) % 8 == 0:
                    dve.wait_ge(*upto("unit_used", in_units + ET * (n + 1) // 8))
                else:
                    dve.wait_ge(*upto("out_ps", n // 2 + 1))
                if n % 2 == 0:
                    dve.wait_ge(sem(f"res_in{n // 2 % 2}"), 16 * (n // 4 + 1))
                V.tensor_tensor(halves(fin[:, n, :]), proj_ps(NTILE + n), halves(fin[:, n, :]), ALU.add).then_inc(sem("fin_added"), 1)
            elif k == "final":
                dve.wait_ge(*upto("fin_r", 1))
                for n in range(FIN_V):
                    V.tensor_tensor(fin[:, n, :], fin[:, n, :], fin_r[:, :], ALU.mult).then_inc(sem("scaled_v"), 1)

    @block.gpsimd
    def _(pool):
        G = nc.gpsimd

        def split_lo(g, piece):
            if g not in pool_units:
                return
            pool.wait_ge(*upto("w_hi_done", 2 * g + piece + 1))
            s = slice(512 * piece, 512 * piece + 512)
            G.tensor_tensor(w_lo[:, g % 2, s], raw[:, g % NRAW, s], w_hi[:, g % 2, s].bitcast(F32), ALU.subtract).then_inc(sem("w_lo_pool"), 1)

        for it in items:
            k = it[0]
            if k == "proj" and it[2] % 8 in (1, 4):
                g, b = unit_of(it)
                split_lo(g + 1, 0 if b == 1 else 1)
            elif k == "kv":
                split_lo(ring[it] + 1, 0)
                split_lo(ring[it] + 1, 1)
            if k == "xh" and it[1] % 2 == 0:
                kk = it[1]
                pool.wait_ge(*upto("x_hi", kk + 1))
                G.tensor_tensor(h_lo[:, kk, :], x_w[:, 0, :], h_hi[:, kk, :].bitcast(F32), ALU.subtract).then_inc(sem("x_lo_g"), 1)
            elif k == "mh":
                kk = it[1]
                pool.wait_ge(*upto("m_hi", kk + 1))
                G.tensor_tensor(mem_lo[:, kk, :], m_w[:, kk % 2, :], mem_hi[:, kk, :].bitcast(F32), ALU.subtract).then_inc(sem("m_lo"), 1)
            elif k == "post":
                n, s = it[1], it[2]
                kind, i, _ = TILES[n]
                if kind in ("ssd", "gdn") and s == 1:
                    ci, sq = conv_index(n), conv_at[n]
                    if sq == 0:
                        pool.wait_ge(*upto("hist_step", 5))
                        G.tensor_copy(hist3[:, :, :, 0], hist3[:, :, :, 1]).then_inc(sem("hist_moved"), 1)
                        pool.wait_ge(*upto("hist_moved", 1))
                        G.tensor_copy(hist3[:, :, :, 1], hist3[:, :, :, 2]).then_inc(sem("hist_moved"), 1)
                        pool.wait_ge(*upto("hist_moved", 2))
                    pool.wait_ge(*upto("conv_u", sq + 1))
                    G.tensor_copy(tails[:, ci, :], conv_u[:, sq % 2, NT - 3:NT]).then_inc(sem("tail_done"), 1)
                    G.tensor_copy(hist3[:, ci, :, 2], conv_u[:, sq % 2, 0:DB]).then_inc(sem("tail_done"), 1)
                    if sq == NCONV - 1:
                        pool.wait_ge(*upto("tail_done", 2 * NCONV))
                        pool.dma_start(O["tails"], tails[:, :, :]).then_inc(sem("out_tails"), 16)
                        pool.dma_start(O["hist"], hist3[:, :, :, :]).then_inc(sem("out_tails"), 16)
                elif kind == "z" and s == 1:
                    zi, e = z_at[n], i
                    pool.wait_ge(*upto("tile_read", n + 1))
                    G.tensor_copy(z_dec[:, e, :], conv_a[:, zi % 2, 0:DB]).then_inc(sem("z_dec"), 1)
            elif k == "ssd" and 2 <= it[2] <= 5:
                i = 4 * it[1] + it[2] - 2
                pool.wait_ge(*upto("s_sub", i + 1))
                G.affine_select(out=s_l[:, i % 2, :, :], in_=s_l[:, i % 2, :, :], compare_op=ALU.is_ge, fill=-1e30, base=0,
                                pattern=[[0, 4], [1, P]], channel_multiplier=-1).then_inc(sem("s_masked"), 1)
            elif k == "gdn" and it[2] == 1:
                h = it[1]
                for j, (e, first) in enumerate(((g_e1, -1), (g_e2, 0))):
                    pool.wait_ge(*upto("g_sub", 2 * h + j + 1))
                    G.affine_select(out=e[:, :, :], in_=e[:, :, :], compare_op=ALU.is_ge, fill=-1e30, base=first,
                                    pattern=[[0, NC], [1, P]], channel_multiplier=-1).then_inc(sem("g_masked"), 1)
            elif k == "gdn" and 2 <= it[2] < 14 and it[2] % 2 == 0:
                h, s = it[1], it[2]
                if s == 2:
                    if h == 0:
                        pool.wait_ge(*upto("masks_done", 1))
                    pool.wait_ge(*upto("g_nat", h + 1))
                for level in (0, 1) if s == 2 else (s // 2,):
                    if level == 1:
                        pool.wait_ge(*upto("g_attn", h + 1))
                    elif level == 2:
                        pool.wait_ge(*upto("g_t0_ps", h + 1))
                        pool.wait_ge(*upto("g_tt0", h + 1))
                    elif level > 2:
                        pool.wait_ge(*upto("g_at", 6 * h + level - 2))
                    G.tensor_tensor(g_natm[level % 2][:, :, :], g_natf[:, :, :], across(masks[:, level, :], NC), ALU.mult).then_inc(sem("g_natm"), 1)
            elif k == "decssd":
                i = it[1]
                st = d_st[:, i % 4, :, :]
                pool.wait_ge(sem(f"st_in{i % 4}"), 16 * (i // 4 + 1))
                if i == 0:
                    pool.wait_ge(*upto("d_dtx", 1))
                G.tensor_tensor(st, st, along(d_k[:, 1, i, :], P), ALU.mult).then_inc(sem("d_decayed"), 1)
                if i % 4 == 0:
                    pool.wait_ge(*upto("d_bb", 2 * (i // 4) + 1))
                if i:
                    pool.wait_ge(*upto("d_new", i))
                G.tensor_tensor(d_tmp[:, :, :], d_bb[:, 0, :, :], along(d_k[:, 2, i, :], P), ALU.mult).then_inc(sem("d_outer1"), 1)
            elif k == "decgdn0":
                pool.wait_ge(*upto("d_ymul", 8))
                G.memset(q_sel[:, :], 0.0).then_inc(sem("sel_zero"), 1)
            elif k == "decattk" and it[1] == 0:
                pool.wait_ge(*upto("d_new", 8 + GDN_H))
                G.memset(p_sel[:, :, :], 0.0).then_inc(sem("sel_zero"), 1)
            elif k == "decgdn" and it[2] == 0:
                h = it[1]
                st = d_st[:, h % 4, :, :]
                pool.wait_ge(*upto("d_ks", h + 1))
                if h == 0:
                    pool.wait_ge(*upto("d_g", 1))
                G.tensor_tensor(st, st, along(d_g[:, 2, h, :], P), ALU.mult).then_inc(sem("d_decayed"), 1)
            elif k == "ylo" and it[1] % 2 == 0:
                e = it[1]
                if e == 0:
                    pool.wait_ge(*upto("unit_used", in_units))
                pool.wait_ge(*upto("y_hi_done", e + 1))
                G.tensor_tensor(y_lo[:, SLOT[e], :], y_raw[:, SLOT[e], :], y_hi[:, SLOT[e], :].bitcast(F32), ALU.subtract).then_inc(sem("y_lo_g"), 1)
            elif k == "fin" and it[2] == 3 and it[1] < KT - 1:
                n = it[1]
                pool.wait_ge(*upto("fin_sq", n + 1))
                if n == 0:
                    G.tensor_copy(fin_acc[:, :], fin_sq[:, 0, :]).then_inc(sem("fin_acc"), 1)
                else:
                    pool.wait_ge(*upto("fin_acc", n))
                    G.tensor_tensor(fin_acc[:, :], fin_acc[:, :], fin_sq[:, n % 2, :], ALU.add).then_inc(sem("fin_acc"), 1)
            elif k == "final":
                pool.wait_ge(*upto("fin_r", 1))
                for n in range(FIN_V, KT):
                    G.tensor_tensor(fin[:, n, :], fin[:, n, :], fin_r[:, :], ALU.mult).then_inc(sem("scaled_g"), 1)

    ctx.close()


def kernel(**inputs):
    import concourse.bacc as bacc
    from concourse.bass_utils import run_bass_kernel_spmd

    A = {k: np.asarray(v) for k, v in inputs.items()}

    def blocks_of(w):
        return w.reshape(-1, P, w.shape[1]).transpose(1, 0, 2)

    x_rows, x_dec, mem = A["x_prompt"][0], A["x_sample"][:, 0], A["mem_prompt"][0]
    w_in = blocks_of(A["w_in"][0])
    units_in = np.stack([w_in[:, 8 * half:8 * half + 8, c0:c0 + P].reshape(P, UNIT)
                         for _, _, c0 in TILES for half in range(2)])
    w_out = blocks_of(A["w_out"][0])
    units_out = w_out.reshape(P, ET, KT, P).transpose(2, 1, 0, 3).reshape(KT * ET // 8, 8, P, P).transpose(0, 2, 1, 3).reshape(-1, P, UNIT)
    rows = lambda v: np.broadcast_to(v.reshape(1, -1), (P, v.size))
    cols = lambda v: v.reshape(-1, P).T
    conv_w = np.concatenate([A["ssd_conv_w"][0], A["gdn_conv_w"][0]], 1).reshape(CW, NCONV, P).transpose(2, 1, 0)
    no_bias = np.zeros(GDN_H, np.float32)
    gdn_a = A["gdn_A_log"][0]
    vecs = np.concatenate([
        cols(A["norm_w"][0]), cols(A["mem_norm_w"][0]), cols(A["mix_norm_w"][0]), conv_w.reshape(P, -1),
        cols(A["ssd_conv_b"][0]),
        rows(np.concatenate([A["ssd_dt_bias"][0], no_bias, A["gdn_dt_bias"][0]])),
        rows(np.concatenate([A["ssd_A_log"][0], gdn_a, gdn_a])), rows(A["ssd_D"][0]),
        np.repeat(A["ssd_D"][0].reshape(8, 2), SSD_P, axis=1).T], axis=1)
    i = np.arange(P)
    csts = np.stack([i[:, None] <= i, np.ones((P, P)), i[:, None] // SSD_P == i // SSD_P], 1)
    masks = []
    for s in LEVELS:
        m = (i[:, None] // (2 * s) == i // (2 * s)) & (i[:, None] // s % 2 == 1) & (i // s % 2 == 0)
        masks.append(m.T)
    hist = np.concatenate([A["state_ssd_conv"][0], A["state_gdn_conv"][0]], 2)
    ins = {
        "x_t": np.concatenate([x_dec, x_rows]).T.reshape(KT, P, NT).transpose(1, 0, 2),
        "mem_t": mem.T.reshape(KT, P, MEM_T).transpose(1, 0, 2),
        "w_mem": A["w_mem_kv"][0].reshape(KT, P, UNIT), "w_in": units_in, "w_out": units_out,
        "w_small": np.concatenate([w_in[:, :, COL_DT:COL_DT + SSD_H], w_in[:, :, COL_B:COL_B + 2 * GDN_H]], 2),
        "vecs": vecs, "csts": csts.astype(np.float32), "ident": np.eye(P, dtype=np.float32), "masks": np.stack(masks, 1).astype(np.float32),
        "hist": hist.reshape(DB, 3, NCONV, P).transpose(3, 2, 0, 1),
        "st_ssd": A["state_ssd"][0].reshape(DB, 8, P, SSD_N).transpose(1, 2, 0, 3),
        "st_gdn": A["state_gdn"][0].transpose(1, 2, 0, 3),
        "c_k": A["cache_mem_k"][0].transpose(0, 3, 2, 1).reshape(DB, P, 8, P),
        "c_v": A["cache_mem_v"][0].reshape(DB, 2, P, MEM_H, P).transpose(0, 2, 1, 3, 4).reshape(DB, P, 8, P),
        "final_w": cols(A["final_norm_w"]),
    }
    ins = {k: np.ascontiguousarray(v) for k, v in ins.items()}
    outs = {
        "y_t": (P, KT, NT), "tails": (P, NCONV, 3), "hist": (P, NCONV, DB, 3),
        "p_ssd": (P, SSD_W), "p_gdn": (GDN_H, P, P), "p_mem_k": (P, MEM_H, MEM_T), "p_mem_v": (P, 2, MEM_W),
        "s_ssd": (8, P, DB, P), "s_gdn": (GDN_H, P, DB, P),
    }
    nc = bacc.Bacc("TRN2", target_bir_lowering=False, num_devices=1)
    I = {k: nc.dram_tensor("in_" + k, v.shape, mybir.dt.from_np(v.dtype), kind="ExternalInput").ap() for k, v in ins.items()}
    O = {k: nc.dram_tensor("out_" + k, s, F32, kind="ExternalOutput").ap() for k, s in outs.items()}
    build(nc, I, O)
    r = run_bass_kernel_spmd(nc, [{"in_" + k: v for k, v in ins.items()}], core_ids=[0]).results[0]
    r = {k: np.asarray(r["out_" + k]) for k in outs}

    y = r["y_t"].transpose(2, 1, 0).reshape(NT, D)
    tails = r["tails"].transpose(2, 1, 0).reshape(1, 1, 3, NCONV * P)
    hist = r["hist"].transpose(2, 3, 1, 0).reshape(1, DB, 3, NCONV * P)
    return (
        y[None, DB:], y[:DB, None],
        tails[..., :SSD_CONV], r["p_ssd"].T.reshape(1, 1, SSD_H, SSD_P, SSD_N),
        tails[..., SSD_CONV:], r["p_gdn"][None, None],
        r["p_mem_k"].transpose(2, 1, 0)[None, None],
        r["p_mem_v"].transpose(1, 0, 2).reshape(1, 1, MEM_T, MEM_H, P),
        hist[..., :SSD_CONV], r["s_ssd"].transpose(2, 0, 1, 3).reshape(1, DB, SSD_H, SSD_P, SSD_N),
        hist[..., SSD_CONV:], r["s_gdn"].transpose(2, 0, 1, 3)[None],
    )
```
